# Optimizing a Trainium2 kernel written in Bass

```python
import math
import jax, jax.numpy as jnp
from jax import lax
import numpy as np

D_MODEL = 1024
BATCH = 1
SEQ = 256
DEPTH = 2

GLA_HEADS = 4
GLA_DK = 64
GLA_DV = 128
GLA_RANK = 16
GLA_GATE_TEMP = 16.0
GLA_CHUNK = 64
DIL_HEADS = 8
DIL_DH = 64
DIL_PATTERNS = ((128, 1), (512, 4), (2048, 16))
DIL_BLOCK = 128
MLSTM_HEADS = 4
MLSTM_DH = 128
MLSTM_CHUNK = 64
MLSTM_CONV = 4
D_FF = 2816
N_BRANCH = 3
DN_ALPHA = (2 * DEPTH) ** 0.25
DN_BETA = (8 * DEPTH) ** -0.25
LN_EPS = 1e-5

GLA_QK_W = GLA_HEADS * GLA_DK
GLA_V_W = GLA_HEADS * GLA_DV
DIL_W = DIL_HEADS * DIL_DH
ML_W = MLSTM_HEADS * MLSTM_DH
IN_WIDTHS = (GLA_QK_W, GLA_QK_W, GLA_V_W, GLA_V_W, GLA_RANK,
             DIL_W, DIL_W, DIL_W,
             ML_W, ML_W, ML_W, MLSTM_HEADS, MLSTM_HEADS, ML_W,
             N_BRANCH * D_MODEL)
D_IN = sum(IN_WIDTHS)

kernel_name = "hybrid_gla_dilated_mlstm_macaron_deepnorm"

def layer_norm(x, g, b):
    xf = x.astype(jnp.float32)
    mu = jnp.mean(xf, -1, keepdims=True)
    var = jnp.mean(jnp.square(xf - mu), -1, keepdims=True)
    return ((xf - mu) * lax.rsqrt(var + LN_EPS) * g + b).astype(x.dtype)

def head_group_norm(h, g):
    mu = jnp.mean(h, -1, keepdims=True)
    var = jnp.mean(jnp.square(h - mu), -1, keepdims=True)
    hn = (h - mu) * lax.rsqrt(var + LN_EPS)
    return hn.reshape(h.shape[0], h.shape[1], -1) * g.astype(jnp.float32)

def swiglu(x, w_gate, w_up, w_down):
    return (jax.nn.silu(x @ w_gate) * (x @ w_up)) @ w_down

def causal_depthwise_conv(x, w, b):
    K, C = w.shape
    y = lax.conv_general_dilated(x, w[:, None, :], window_strides=(1,), padding=[(K - 1, 0)],
                                 dimension_numbers=('NWC', 'WIO', 'NWC'), feature_group_count=C)
    return y + b

def gla_mixer(q, k, v, r, a_low, w_a2, b_a, g_norm):
    B_, S_, _ = q.shape
    L = GLA_CHUNK
    nc = S_ // L
    f32 = jnp.float32
    log_a = jax.nn.log_sigmoid((a_low @ w_a2 + b_a).astype(f32)) / GLA_GATE_TEMP

    def chunks(t, d):
        return t.astype(f32).reshape(B_, nc, L, GLA_HEADS, d).transpose(0, 3, 1, 2, 4)

    qc = chunks(q, GLA_DK) * GLA_DK ** -0.5
    kc = chunks(k, GLA_DK)
    vc = chunks(v, GLA_DV)
    bc = jnp.cumsum(chunks(log_a, GLA_DK), axis=3)
    b_last = bc[..., -1:, :]
    q_dec = qc * jnp.exp(bc)
    k_inv = kc * jnp.exp(-bc)
    causal = jnp.tril(jnp.ones((L, L), bool))
    att = jnp.where(causal, jnp.einsum('bhctk,bhcsk->bhcts', q_dec, k_inv), 0.0)
    o_intra = jnp.einsum('bhcts,bhcsv->bhctv', att, vc)
    kv_chunk = jnp.einsum('bhcsk,bhcsv->bhckv', kc * jnp.exp(b_last - bc), vc)
    decay = jnp.exp(b_last[..., 0, :])

    def step(state, inp):
        dec, kv = inp
        return dec[..., None] * state + kv, state

    s0 = jnp.zeros((B_, GLA_HEADS, GLA_DK, GLA_DV), f32)
    _, s_prev = lax.scan(step, s0, (jnp.moveaxis(decay, 2, 0), jnp.moveaxis(kv_chunk, 2, 0)))
    s_prev = jnp.moveaxis(s_prev, 0, 2)
    o = o_intra + jnp.einsum('bhctk,bhckv->bhctv', q_dec, s_prev)
    o = o.transpose(0, 2, 3, 1, 4).reshape(B_, S_, GLA_HEADS, GLA_DV)
    y = head_group_norm(o, g_norm) * jax.nn.silu(r.astype(f32))
    return y.astype(q.dtype)

def _strided_window_attention(qh, kh, vh, n_back, dil, slopes):
    B_, S_, H, dh = qh.shape
    f32 = jnp.float32
    BLK = DIL_BLOCK
    Ls = S_ // dil
    nb = -(-Ls // BLK)
    Lp = nb * BLK

    def sub(t):
        t = t.astype(f32).reshape(B_, Ls, dil, H, dh).transpose(0, 2, 3, 1, 4)
        t = jnp.pad(t, ((0, 0), (0, 0), (0, 0), (0, Lp - Ls), (0, 0)))
        return t.reshape(B_, dil, H, nb, BLK, dh)

    def with_prev(t):
        prev = jnp.pad(t, ((0, 0), (0, 0), (0, 0), (1, 0), (0, 0), (0, 0)))[:, :, :, :-1]
        return jnp.concatenate([prev, t], axis=4)

    qb = sub(qh) * dh ** -0.5
    kcat = with_prev(sub(kh))
    vcat = with_prev(sub(vh))
    qpos = jnp.arange(nb)[:, None, None] * BLK + jnp.arange(BLK)[None, :, None]
    kpos = jnp.arange(nb)[:, None, None] * BLK + jnp.arange(2 * BLK)[None, None, :] - BLK
    dist = qpos - kpos
    valid = (dist >= 0) & (dist <= n_back) & (kpos >= 0)
    bias = -slopes[:, None, None, None] * (dist * dil).astype(f32)[None]
    s = jnp.einsum('bdhnqe,bdhnke->bdhnqk', qb, kcat) + bias
    s = jnp.where(valid, s, -jnp.inf)
    lse = jax.nn.logsumexp(s, axis=-1)
    p = jnp.exp(s - lse[..., None])
    o = jnp.einsum('bdhnqk,bdhnke->bdhnqe', p, vcat)
    o = o.reshape(B_, dil, H, Lp, dh)[:, :, :, :Ls].transpose(0, 3, 1, 2, 4).reshape(B_, S_, H, dh)
    lse = lse.reshape(B_, dil, H, Lp)[..., :Ls].transpose(0, 3, 1, 2).reshape(B_, S_, H)
    return o, lse

def dilated_attention(q, k, v):
    B_, S_, _ = q.shape
    shp = (B_, S_, DIL_HEADS, DIL_DH)
    qh, kh, vh = q.reshape(shp), k.reshape(shp), v.reshape(shp)
    slopes = 2.0 ** (-8.0 * jnp.arange(1, DIL_HEADS + 1, dtype=jnp.float32) / DIL_HEADS)
    outs, lses = [], []
    for window, dil in DIL_PATTERNS:
        o, lse = _strided_window_attention(qh, kh, vh, window // dil, dil, slopes)
        outs.append(o)
        lses.append(lse)
    w = jax.nn.softmax(jnp.stack(lses, 0), axis=0)
    out = jnp.sum(w[..., None] * jnp.stack(outs, 0), axis=0)
    return out.reshape(B_, S_, DIL_W).astype(q.dtype)

def mlstm_mixer(q, k, v, i_pre, f_pre, o_pre, g_norm):
    B_, S_, _ = q.shape
    L = MLSTM_CHUNK
    nc = S_ // L
    H, dh = MLSTM_HEADS, MLSTM_DH
    f32 = jnp.float32

    def chunks(t):
        return t.astype(f32).reshape(B_, nc, L, H, dh).transpose(0, 3, 1, 2, 4)

    def gchunks(t):
        return t.astype(f32).reshape(B_, nc, L, H).transpose(0, 3, 1, 2)

    qc, kc, vc = chunks(q), chunks(k) * dh ** -0.5, chunks(v)
    log_i = gchunks(i_pre)
    F = jnp.cumsum(jax.nn.log_sigmoid(gchunks(f_pre)), axis=-1)
    F_last = F[..., -1]
    causal = jnp.tril(jnp.ones((L, L), bool))
    Dlog = jnp.where(causal, F[..., :, None] - F[..., None, :] + log_i[..., None, :], -jnp.inf)
    m_intra = jnp.max(Dlog, axis=-1)
    P = jnp.exp(Dlog - m_intra[..., None])
    Sqk = jnp.einsum('bhctd,bhcsd->bhcts', qc, kc) * P
    num_intra = jnp.einsum('bhcts,bhcsd->bhctd', Sqk, vc)
    den_intra = jnp.sum(Sqk, axis=-1)
    g = F_last[..., None] - F + log_i
    m_chunk = jnp.max(g, axis=-1)
    wgt = jnp.exp(g - m_chunk[..., None])
    kv_chunk = jnp.einsum('bhcs,bhcsv,bhcsk->bhcvk', wgt, vc, kc)
    n_chunk = jnp.einsum('bhcs,bhcsk->bhck', wgt, kc)

    def step(carry, inp):
        C, n, m = carry
        fl, mc, kv, nk = inp
        m_new = jnp.maximum(fl + m, mc)
        a = jnp.exp(fl + m - m_new)
        b = jnp.exp(mc - m_new)
        return (a[..., None, None] * C + b[..., None, None] * kv, a[..., None] * n + b[..., None] * nk, m_new), (C, n, m)

    init = (jnp.zeros((B_, H, dh, dh), f32), jnp.zeros((B_, H, dh), f32), jnp.zeros((B_, H), f32))
    xs = (jnp.moveaxis(F_last, 2, 0), jnp.moveaxis(m_chunk, 2, 0),
          jnp.moveaxis(kv_chunk, 2, 0), jnp.moveaxis(n_chunk, 2, 0))
    _, (C_prev, n_prev, m_prev) = lax.scan(step, init, xs)
    C_prev = jnp.moveaxis(C_prev, 0, 2)
    n_prev = jnp.moveaxis(n_prev, 0, 2)
    m_prev = jnp.moveaxis(m_prev, 0, 2)
    a_t = F + m_prev[..., None]
    m_t = jnp.maximum(a_t, m_intra)
    w_inter = jnp.exp(a_t - m_t)
    w_intra = jnp.exp(m_intra - m_t)
    num = w_inter[..., None] * jnp.einsum('bhcvk,bhctk->bhctv', C_prev, qc) + w_intra[..., None] * num_intra
    den = w_inter * jnp.einsum('bhck,bhctk->bhct', n_prev, qc) + w_intra * den_intra
    h = num / jnp.maximum(jnp.abs(den), jnp.exp(-m_t))[..., None]
    h = h.transpose(0, 2, 3, 1, 4).reshape(B_, S_, H, dh)
    y = head_group_norm(h, g_norm) * jax.nn.sigmoid(o_pre.astype(f32))
    return y.astype(q.dtype)

def hybrid_mixer(x, w_in, gla_w_a2, gla_b_a, gla_norm_g, ml_conv_w, ml_conv_b, ml_b_i, ml_b_f,
                 ml_norm_g, w_proj_gla, w_proj_dil, w_proj_ml, b_gate, w_out):
    B_, S_, D = x.shape
    z = x @ w_in
    split_points = np.cumsum(IN_WIDTHS)[:-1].tolist()
    (gq, gk, gv, gr, ga, dq, dk, dv, mq, mk, mv, mi, mf, mo, gates) = jnp.split(z, split_points, axis=-1)
    y_gla = gla_mixer(gq, gk, gv, gr, ga, gla_w_a2, gla_b_a, gla_norm_g)
    y_dil = dilated_attention(dq, dk, dv)
    mqk = jax.nn.silu(causal_depthwise_conv(jnp.concatenate([mq, mk], -1), ml_conv_w, ml_conv_b))
    mq, mk = jnp.split(mqk, 2, axis=-1)
    y_ml = mlstm_mixer(mq, mk, mv, mi + ml_b_i, mf + ml_b_f, mo, ml_norm_g)
    g = jax.nn.sigmoid(gates + b_gate).reshape(B_, S_, N_BRANCH, D)
    merged = (g[..., 0, :] * (y_gla @ w_proj_gla) + g[..., 1, :] * (y_dil @ w_proj_dil)
              + g[..., 2, :] * (y_ml @ w_proj_ml))
    return merged @ w_out

def setup_inputs(seed: int = 0) -> dict:
    key = jax.random.key(seed)
    ks = iter(jax.random.split(key, 32))

    def nrm(shape, scale):
        return jax.random.normal(next(ks), shape, jnp.float32) * scale

    L, D = DEPTH, D_MODEL
    return {
        "x": nrm((BATCH, SEQ, D), 1.0),
        "ffn1_w_gate": nrm((L, D, D_FF), D ** -0.5),
        "ffn1_w_up": nrm((L, D, D_FF), D ** -0.5),
        "ffn1_w_down": nrm((L, D_FF, D), D_FF ** -0.5 * DN_BETA),
        "ln1_g": 1.0 + nrm((L, D), 0.02),
        "ln1_b": nrm((L, D), 0.02),
        "w_in": nrm((L, D, D_IN), D ** -0.5),
        "gla_w_a2": nrm((L, GLA_RANK, GLA_QK_W), GLA_RANK ** -0.5),
        "gla_b_a": nrm((L, GLA_QK_W), 0.1),
        "gla_norm_g": 1.0 + nrm((L, GLA_V_W), 0.02),
        "ml_conv_w": nrm((L, MLSTM_CONV, 2 * ML_W), MLSTM_CONV ** -0.5),
        "ml_conv_b": nrm((L, 2 * ML_W), 0.02),
        "ml_b_i": nrm((L, MLSTM_HEADS), 0.1),
        "ml_b_f": 3.0 + nrm((L, MLSTM_HEADS), 0.5),
        "ml_norm_g": 1.0 + nrm((L, ML_W), 0.02),
        "w_proj_gla": nrm((L, GLA_V_W, D), GLA_V_W ** -0.5),
        "w_proj_dil": nrm((L, DIL_W, D), DIL_W ** -0.5),
        "w_proj_ml": nrm((L, ML_W, D), ML_W ** -0.5),
        "b_gate": nrm((L, N_BRANCH * D), 0.02),
        "w_out": nrm((L, D, D), D ** -0.5 * DN_BETA),
        "ln2_g": 1.0 + nrm((L, D), 0.02),
        "ln2_b": nrm((L, D), 0.02),
        "ffn2_w_gate": nrm((L, D, D_FF), D ** -0.5),
        "ffn2_w_up": nrm((L, D, D_FF), D ** -0.5),
        "ffn2_w_down": nrm((L, D_FF, D), D_FF ** -0.5 * DN_BETA),
        "ln3_g": 1.0 + nrm((L, D), 0.02),
        "ln3_b": nrm((L, D), 0.02),
    }

def reference(x, ffn1_w_gate, ffn1_w_up, ffn1_w_down, ln1_g, ln1_b, w_in, gla_w_a2, gla_b_a,
              gla_norm_g, ml_conv_w, ml_conv_b, ml_b_i, ml_b_f, ml_norm_g, w_proj_gla, w_proj_dil,
              w_proj_ml, b_gate, w_out, ln2_g, ln2_b, ffn2_w_gate, ffn2_w_up, ffn2_w_down, ln3_g, ln3_b):
    for l in range(DEPTH):
        x = layer_norm(DN_ALPHA * x + 0.5 * swiglu(x, ffn1_w_gate[l], ffn1_w_up[l], ffn1_w_down[l]),
                       ln1_g[l], ln1_b[l])
        mix = hybrid_mixer(x, w_in[l], gla_w_a2[l], gla_b_a[l], gla_norm_g[l], ml_conv_w[l], ml_conv_b[l],
                           ml_b_i[l], ml_b_f[l], ml_norm_g[l], w_proj_gla[l], w_proj_dil[l], w_proj_ml[l],
                           b_gate[l], w_out[l])
        x = layer_norm(DN_ALPHA * x + mix, ln2_g[l], ln2_b[l])
        x = layer_norm(DN_ALPHA * x + 0.5 * swiglu(x, ffn2_w_gate[l], ffn2_w_up[l], ffn2_w_down[l]),
                       ln3_g[l], ln3_b[l])
    return x


_drawn_inputs = setup_inputs


def setup_inputs(seed=0):
    import zlib

    import numpy as np

    out = dict(_drawn_inputs(seed))
    spreads = {}
    factors = {'gla_w_a2': 3.341,
     'gla_b_a': 8.0,
     'gla_norm_g': 21.464,
     'ml_conv_b': 8.0,
     'ml_b_i': 64.0,
     'ml_norm_g': 22.496,
     'b_gate': 8.0}
    for name, (base, spread) in spreads.items():
        noise = np.random.default_rng([zlib.crc32(name.encode()), seed]).standard_normal(out[name].shape)
        drawn = base * np.exp(spread * noise) if base else spread * noise
        out[name] = __import__('jax').numpy.asarray(drawn.astype(out[name].dtype))
    for name, factor in factors.items():
        out[name] = (out[name] * factor).astype(out[name].dtype)
    return out
```

```python
from contextlib import ExitStack

import numpy as np

import concourse.bass as bass
from concourse import mybir

ALU = mybir.AluOpType
ACT = mybir.ActivationFunctionType
F32 = mybir.dt.float32
F32R = mybir.dt.float32r
I32 = mybir.dt.int32
AX = mybir.AxisListType.X

P = 128
LAYERS, SEQ, D, FF = 2, 256, 1024, 2816
TT = SEQ // P
KD = D // P
LC = 64
NC = SEQ // LC
GH, GK, GV, RANK = 4, 64, 128, 16
DH, DE = 8, 64
MH, ME = 4, 128
CONV = 4
EPS = 1e-5
ALPHA = float((2 * LAYERS) ** 0.25)
BIG = 1e30

FG = 256
NG = FF // FG
SLOTS = 3
BW = 2048
FB = 3 * NG
NGRP = 16
B_MIX = FB
B_PROJ = B_MIX + 2 * NGRP
B_OUT = B_PROJ + 6
B_FFN2 = B_OUT + 4
BLOCKS = B_FFN2 + FB
assert B_MIX % SLOTS == 0 and B_FFN2 % SLOTS == 0 and BLOCKS % SLOTS == 0
SM = 68
(G_GQK, G_GV, G_GR, G_DQ, G_DK, G_DV, G_MQ, G_MK, G_MV, G_MO, G_GATE) = range(11)

GATE_GRPS = NGRP - G_GATE

C_ID, C_TRI, C_SUF, C_BIG, C_DIST, C_LNC, C_SEL = 0, 128, 256, 384, 512, 896, 1280
C_W = C_SEL + MH * P
V_GG, V_MG, V_BA, V_W = 0, 512, 1024, 1280


def trunk(nc, x_in, stream, consts, lnp, vecs, bgate, wsmall, wa2, bif, convp, out):
    with ExitStack() as ctx:
        def sb(name, shape, dt=F32):
            return ctx.enter_context(nc.sbuf_tensor(name, shape, dt))

        def sem(name):
            return ctx.enter_context(nc.semaphore(name))

        raw = sb("raw", [P, SLOTS, BW])
        hi = sb("hi", [P, SLOTS, BW], F32R)
        lo = sb("lo", [P, SLOTS, BW], F32R)
        X = sb("X", [P, TT, D])
        U = sb("U", [P, TT, D])
        xTh = sb("xTh", [P, KD, SEQ], F32R)
        xTl = sb("xTl", [P, KD, SEQ], F32R)
        hTh = sb("hTh", [P, KD * SM], F32R)
        hTl = sb("hTl", [P, KD * SM], F32R)
        fscr = sb("fscr", [P, MH * (CONV - 1 + SEQ)])
        fsil = fscr[:, 0:TT * FG].rearrange("p (t n) -> p t n", t=TT)
        fh = fscr[:, TT * FG:2 * TT * FG].rearrange("p (t n) -> p t n", t=TT)
        cin = fscr[:, :].rearrange("p (h n) -> p h n", h=MH)
        pln = sb("pln", [P, 2 * D])
        vec = sb("vec", [P, V_W])
        bg = sb("bg", [P, 2, 512])
        cst = sb("cst", [P, C_W])
        cvp = sb("cvp", [P, 2 * MH, CONV + 1])
        bif_t = sb("bif_t", [MH, 2])
        gates = sb("gates", [P, TT, 3 * D])
        gv = sb("gv", [P, TT, 512])
        gr = sb("gr", [P, TT, 512])
        dv = sb("dv", [P, TT, 512])
        mv1 = sb("mv1", [P, TT, MH, ME + 1])
        mo = sb("mo", [P, TT, 512])
        R2 = sb("R2", [P, 4644])
        bh = sb("bh", [P, 384])
        emr = sb("emr", [MH, SEQ])
        small = sb("small", [P, 256])
        qkT = pln[:, :].rearrange("p (j n) -> p j n", j=2 * MH)
        T0 = U[:, 0, :].rearrange("p (t n) -> p t n", t=TT)
        T1 = U[:, 1, :].rearrange("p (t n) -> p t n", t=TT)
        gscr = gates[:, :, :].rearrange("p t n -> p (t n)")
        la, le = gscr[:, 0:512], gscr[:, 512:1024]
        E1, E2, E3 = (gscr[:, 1024 + 512 * i:1536 + 512 * i] for i in range(3))
        qdT, kiT, kd = (gscr[:, 2560 + 512 * i:3072 + 512 * i] for i in range(3))
        attm = gscr[:, 4096:5120].rearrange("p (q n) -> p q n", q=2)
        gst = gscr[:, 5120:5888].rearrange("p (c a n) -> p c a n", c=NC - 1, a=2)
        aT = gscr[0:RANK, 5888:6144]
        gyn = gscr[:, 1024:2048].rearrange("p (t n) -> p t n", t=TT)
        dqT = R2[:, 0:1024].rearrange("p (a n) -> p a n", a=4)
        dkT = R2[:, 1024:2048].rearrange("p (a n) -> p a n", a=4)
        dL, dPT = R2[:, 2048:2432], R2[:, 2432:2816]
        wsm_raw = R2[:, 0:KD * SM]
        wa2_t = R2[0:RANK, 544:800]
        G_, gf, F_, M_, WI, WK = (R2[0:MH, 3096 + 256 * i:3352 + 256 * i] for i in range(6))
        EM = emr[:, :]
        mA = R2[:, 0:1024].rearrange("p (t n) -> p t n", t=TT)
        mkw = R2[:, 1024:2048].rearrange("p (t n) -> p t n", t=TT)
        qwT = R2[:, 2048:3072].rearrange("p (h n) -> p h n", h=MH)
        mcs = R2[:, 3096:3096 + 3 * MH * (ME + 1)].rearrange("p (c h n) -> p c h n", c=NC - 1, h=MH)
        st = small[:, 0:48].rearrange("p (a n) -> p a n", n=6)
        mv = small[:, 48:64].rearrange("p (a n) -> p a n", n=2)
        vv, rs, rt = small[:, 64:72], small[:, 72:80], small[:, 80:88]
        dmax = small[:, 88:90]
        dsum = small[:, 90:106].rearrange("p (t h) -> p t h", t=TT)
        drec = small[:, 106:122].rearrange("p (t h) -> p t h", t=TT)
        mc = small[:, 122:154].rearrange("p (t q h) -> p t q h", t=TT, q=4)
        ac = small[:, 154:170].rearrange("p (h c) -> p h c", h=MH)
        rden = small[:, 170:172]
        mprev = small[0:MH, 172:172 + NC + 1]
        ones4 = small[0:MH, 180:180 + LC]
        ident = cst[:, C_ID:C_ID + P]
        tri = cst[:, C_TRI:C_TRI + P]
        B = [ctx.enter_context(nc.psum_tensor(f"bank{i}", [P, 512], F32)) for i in range(8)]

        s_x_in = sem("x_loaded")
        s_cst = sem("consts_loaded")
        s_par = sem("layer_params_loaded")
        s_pln = sem("norm_params_loaded")
        s_bg = [sem(f"gate_bias_loaded{i}") for i in range(2)]
        s_raw = [sem(f"raw_loaded{i}") for i in range(SLOTS)]
        s_hi = sem("hi_split")
        s_lo = sem("lo_split")
        s_used = sem("block_used")
        s_x = sem("x_ready")
        s_xt = sem("x_transposed")
        s_xh = sem("xT_hi")
        s_xl = sem("xT_lo")
        s_gu = sem("gate_up_done")
        s_sil = sem("silu_done")
        s_h = sem("h_ready")
        s_ht = sem("h_transposed")
        s_hh = sem("hT_hi")
        s_hl = sem("hT_lo")
        s_acc = sem("sublayer_done")
        s_out = sem("out_stored")
        s_small_ps = sem("small_ps")
        s_gla_gate_ps = sem("gla_gate_ps")
        s_gla_cum = sem("gla_cum")
        s_gla_scores = sem("gla_scores")
        s_gla_out = sem("gla_out")
        s_dil_q_T = sem("dil_q_T")
        s_dil_k_T = sem("dil_k_T")
        s_ml_q_T = sem("ml_q_T")
        s_ml_k_T = sem("ml_k_T")
        s_ml_cols = sem("ml_cols")
        s_ml_max_b = sem("ml_max_b")
        s_ml_scores = sem("ml_scores")
        s_ml_k_nat = sem("ml_k_nat")
        s_ml_inter_b = sem("ml_inter_b")
        s_ml_kv = sem("ml_kv")
        s_yT = sem("yT")
        s_merged_T = sem("merged_T")
        s_group0 = sem("group0")
        s_dil_pv = sem("dil_pv")
        s_dil_p_T = sem("dil_p_T")
        s_dil_scores = sem("dil_scores")
        s_ml_out = sem("ml_out")
        s_small_hi = sem("small_hi")
        s_group_out = sem("group_out")
        s_softplus = sem("softplus")
        s_gla_decay = sem("gla_decay")
        s_ml_rows_exp = sem("ml_rows_exp")
        s_dil_qT = sem("dil_qT")
        s_dil_kT = sem("dil_kT")
        s_conv_in = sem("conv_in")
        s_ml_weights = sem("ml_weights")
        s_y_hi = sem("y_hi")
        s_merged_hi = sem("merged_hi")
        s_gate_sig = sem("gate_sig")
        s_out_gate = sem("out_gate")
        s_dil_pT = sem("dil_pT")
        s_dil_exp = sem("dil_exp")
        s_small_lo = sem("small_lo")
        s_small_out = sem("small_out")
        s_gate_abs = sem("gate_abs")
        s_log_sig = sem("log_sig")
        s_ml_rows = sem("ml_rows")
        s_gla_qk = sem("gla_qk")
        s_gla_state = sem("gla_state")
        s_gla_norm = sem("gla_norm")
        s_dil_y = sem("dil_y")
        s_ml_mc = sem("ml_mc")
        s_conv = sem("conv")
        s_ml_A = sem("ml_A")
        s_ml_q = sem("ml_q")
        s_ml_state = sem("ml_state")
        s_y_lo = sem("y_lo")
        s_merged_lo = sem("merged_lo")
        s_ml_y = sem("ml_y")
        s_merged = sem("merged")
        s_gates_out = sem("gates_out")
        s_dil_logits = sem("dil_logits")
        block = ctx.enter_context(nc.Block())

        def block_used(eng, l, b):
            eng.wait_ge(s_used, BLOCKS * l + (b + 1 + SLOTS))

        def group_tile_done(eng, l, i, tt):
            if tt == 0:
                eng.wait_ge(s_group0, NGRP * l + (i + 1))
            else:
                block_used(eng, l, B_MIX + 2 * i + 1)

        def half_cols(i):
            return slice(512 * i, 512 * i + 512)

        @block.sync
        def _(sp):
            sp.dma_start(X[:, :, :], x_in.rearrange("(t p) n -> p t n", p=P)).then_inc(s_x_in, 16)
            for s in range(SLOTS):
                sp.dma_start(raw[:, s, :], stream[s]).then_inc(s_raw[s], 16)
            sp.dma_start(cst[:, :], consts).then_inc(s_cst, 16)
            with sp.Fori(1, LAYERS * BLOCKS // SLOTS) as i:
                for s in range(SLOTS):
                    sp.wait_ge(s_lo, SLOTS * i + (s - SLOTS + 1))
                    sp.dma_start(raw[:, s, :], stream[SLOTS * i + s]).then_inc(s_raw[s], 16)
            for tt in range(TT):
                sp.wait_ge(s_x, 6 * LAYERS + tt + 1)
                sp.dma_start(out[P * tt:P * tt + P, :], X[:, tt, :]).then_inc(s_out, 16)
            sp.wait_ge(s_out, 16 * TT)

        @block.scalar
        def _(act):
            def split_hi(n, m, s):
                act.wait_ge(s_raw[s], 16 * m + 16)
                act.wait_ge(s_used, n + 1)
                nc.scalar.copy(hi[:, s, :], raw[:, s, :]).then_inc(s_hi, 1)

            def split_layer_hi(l, b):
                split_hi(BLOCKS * l + b, (BLOCKS // SLOTS) * l + b // SLOTS, b % SLOTS)

            def split_xT_hi(r):
                for i in range(2 * TT):
                    tt, hf = i // 2, i % 2
                    act.wait_ge(s_xt, 2 * TT * r + (i + 1))
                    nc.scalar.copy(xTh[:, 4 * hf:4 * hf + 4, P * tt:P * tt + P],
                                   B[i][:, :].rearrange("p (c n) -> p c n", c=4)).then_inc(s_xh, 1)

            def ffn_group(l, f, g, base, splits, peeled=False):
                it = (2 * NG) * l + (NG * f) + g
                n0 = BLOCKS * l + base + SLOTS * g + SLOTS
                for tt in range(TT):
                    if tt == 0:
                        act.wait_ge(s_gu, it + 1)
                    else:
                        act.wait_ge(s_used, n0 + (2 if peeled else 1))
                    nc.scalar.activation(fsil[:, tt, :], B[tt][:, 0:FG], ACT.Silu).then_inc(s_sil, 1)
                m = (BLOCKS // SLOTS) * l + (base // SLOTS + 1) + g
                if splits:
                    split_hi(n0, m, 0)
                act.wait_ge(s_ht, it + 1)
                nc.scalar.copy(hTh[:, 0:512], B[2][:, :]).then_inc(s_hh, 1)
                if splits:
                    split_hi(n0 + 1, m, 1)
                    split_hi(n0 + 2, m, 2)

            def evac_group(l, i):
                dst = {G_GQK: T0, G_GV: gv, G_GR: gr, G_DQ: T1, G_DK: T0, G_DV: dv, G_MQ: T1,
                       G_MK: T0, G_MO: mo}.get(i)
                if i == G_DK:
                    act.wait_ge(s_gla_qk, l + 1)
                if i == G_MQ:
                    act.wait_ge(s_dil_q_T, l + 1)
                if i == G_MK:
                    act.wait_ge(s_dil_k_T, l + 1)
                for tt in range(TT):
                    group_tile_done(act, l, i, tt)
                    ps = B[2 * (i % 2) + tt]
                    if i == G_MV:
                        last = nc.scalar.copy(mv1[:, tt, :, 0:ME], ps[:, :].rearrange("p (h n) -> p h n", h=MH))
                    elif i == G_GR:
                        last = nc.scalar.activation(gr[:, tt, :], ps[:, :], ACT.Silu)
                    else:
                        last = nc.scalar.copy(dst[:, tt, :], ps[:, :])
                last.then_inc(s_group_out, 1)

            def load_gate_bias(l, i):
                act.dma_start(bg[:, i % 2, :],
                              bgate[l, 512 * i:512 * i + 512].partition_broadcast(P)).then_inc(s_bg[i % 2], 16)

            def load_norm(l, q):
                act.dma_start(pln[:, :], lnp[l, q, :].partition_broadcast(P)).then_inc(s_pln, 16)

            with act.Fori(0, LAYERS) as l:
                act.wait_ge(s_x, (3 * TT) * l + TT)
                act.dma_start(vec[:, :], vecs[l].partition_broadcast(P)).then_inc(s_par, 16)
                act.dma_start(wsm_raw, wsmall[l]).then_inc(s_par, 16)
                act.dma_start(wa2_t, wa2[l]).then_inc(s_par, 16)
                act.dma_start(bif_t[:, :], bif[l]).then_inc(s_par, 16)
                act.dma_start(cvp[:, :, :], convp[l]).then_inc(s_par, 16)
                load_norm(l, 0)
                for b in range(SLOTS):
                    split_layer_hi(l, b)
                split_xT_hi(3 * l)
                ffn_group(l, 0, 0, 0, True, peeled=True)
                with act.Fori(1, NG) as g:
                    ffn_group(l, 0, g, 0, True)

                split_xT_hi(3 * l + 1)
                act.wait_ge(s_par, (5 * 16) * l + 80)
                nc.scalar.copy(hTh[:, :], wsm_raw).then_inc(s_small_hi, 1)
                load_gate_bias(l, 0)
                load_gate_bias(l, 1)
                for k in range(2 * NGRP):
                    if k % 2 and k // 2 < G_GATE:
                        evac_group(l, k // 2)
                    if k == 1:
                        act.wait_ge(s_gate_abs, l + 1)
                        nc.scalar.activation(le, le, ACT.Exp, scale=-1.0)
                        nc.scalar.activation(EM, EM, ACT.Exp, scale=-1.0)
                        act.drain()
                        nc.scalar.activation(le, le, ACT.Ln, bias=1.0)
                        nc.scalar.activation(EM, EM, ACT.Ln, bias=1.0).then_inc(s_softplus, 1)
                    if k == 4:
                        act.wait_ge(s_gla_cum, l + 1)
                        s = 1.0 / 16.0
                        nc.scalar.activation(E1, B[4][:, :], ACT.Exp, scale=s)
                        nc.scalar.activation(E2, B[4][:, :], ACT.Exp, scale=-s)
                        nc.scalar.activation(E3, B[5][:, :], ACT.Exp, scale=s).then_inc(s_gla_decay, 1)
                    if k == 5:
                        act.wait_ge(s_ml_rows, l + 1)
                        nc.scalar.activation(WI, WI, ACT.Exp, scale=-1.0)
                        nc.scalar.activation(WK, WK, ACT.Exp)
                        nc.scalar.activation(EM, EM, ACT.Exp, scale=-1.0).then_inc(s_ml_rows_exp, 1)
                    if k in (10, 11):
                        turned, dst, b0, copied = ((s_dil_q_T, dqT, 6, s_dil_qT) if k == 10 else
                                                    (s_dil_k_T, dkT, 4, s_dil_kT))
                        act.wait_ge(turned, l + 1)
                        for tt in range(TT):
                            last = nc.scalar.copy(dst[:, :, P * tt:P * tt + P],
                                                  B[b0 + tt][:, :].rearrange("p (c n) -> p c n", c=4))
                        last.then_inc(copied, 1)
                    h = k - 12
                    if 0 <= h - 1 < DH:
                        act.wait_ge(s_dil_p_T, DH * l + h)
                        nc.scalar.copy(dPT, B[5][:, 0:384]).then_inc(s_dil_pT, 1)
                    if 0 <= h < DH:
                        act.wait_ge(s_dil_logits, DH * l + (h + 1))
                        nc.scalar.activation(dL[:, 0:P], dL[:, 0:P], ACT.Exp, bias=dmax[:, 0:1],
                                             accum_out=dsum[:, 0, h:h + 1])
                        nc.scalar.activation(dL[:, P:3 * P], dL[:, P:3 * P], ACT.Exp,
                                             bias=dmax[:, 1:2], accum_out=dsum[:, 1, h:h + 1]).then_inc(s_dil_exp, 1)
                    if k in (22, 24):
                        act.wait_ge(s_ml_q_T if k == 22 else s_ml_k_T, l + 1)
                        if k == 24:
                            act.wait_ge(s_conv, 2 * l + 1)
                            nc.scalar.activation(qkT[:, 0:MH, :], qkT[:, 0:MH, :], ACT.Silu)
                        for tt in range(TT):
                            last = nc.scalar.copy(cin[:, :, CONV - 1 + P * tt:CONV - 1 + P * tt + P],
                                                  B[4 + tt][:, :].rearrange("p (h n) -> p h n", h=MH))
                        last.then_inc(s_conv_in, 1)
                    if k == 26:
                        act.wait_ge(s_conv, 2 * l + 2)
                        nc.scalar.activation(qkT[:, MH:, :], qkT[:, MH:, :], ACT.Silu)
                        act.wait_ge(s_ml_max_b, l + 1)
                        act.wait_ge(s_ml_mc, l + 1)
                        for tt in range(TT):
                            for hh in range(MH):
                                last = nc.scalar.activation(mA[:, tt, P * hh:P * hh + P],
                                                            B[4 + tt][:, P * hh:P * hh + P], ACT.Exp,
                                                            bias=mc[:, tt, 0, hh:hh + 1], scale=-1.0)
                        last.then_inc(s_ml_weights, 1)
                    if k % 2 and G_GATE <= k // 2 < NGRP - 2:
                        i = k // 2
                        act.wait_ge(s_gates_out, GATE_GRPS * l + (i - G_GATE + 1))
                        load_gate_bias(l, i - G_GATE + 2)
                    if k == 29:
                        act.wait_ge(s_ml_q, l + 1)
                        load_norm(l, 1)
                    split_layer_hi(l, B_MIX + k + SLOTS)

                def split_y_hi(turned, copied, n, i, b0, c0):
                    act.wait_ge(turned, n * l + (i + 1))
                    for tt in range(TT):
                        last = nc.scalar.copy(xTh[:, c0:c0 + 4, P * tt:P * tt + P],
                                              B[b0 + tt][:, :].rearrange("p (c n) -> p c n", c=4))
                    last.then_inc(copied, 1)

                def sigmoid_gates(b):
                    act.wait_ge(s_gates_out, GATE_GRPS * l + (2 * b + 2))
                    nc.scalar.activation(gates[:, :, D * b:D * b + D], gates[:, :, D * b:D * b + D],
                                                    ACT.Sigmoid).then_inc(s_gate_sig, 1)

                split_y_hi(s_yT, s_y_hi, 3, 0, 0, 0)
                split_y_hi(s_yT, s_y_hi, 3, 1, 2, 4)
                sigmoid_gates(0)
                nc.scalar.activation(mo[:, :, :], mo[:, :, :], ACT.Sigmoid).then_inc(s_out_gate, 1)
                split_layer_hi(l, B_PROJ + SLOTS)
                sigmoid_gates(1)
                sigmoid_gates(2)
                for i in range(1, 4):
                    split_layer_hi(l, B_PROJ + SLOTS + i)
                split_y_hi(s_yT, s_y_hi, 3, 2, 4, 0)
                for i in range(4, 6):
                    split_layer_hi(l, B_PROJ + SLOTS + i)
                split_y_hi(s_merged_T, s_merged_hi, 2, 0, 0, 0)
                split_y_hi(s_merged_T, s_merged_hi, 2, 1, 2, 4)
                for i in range(4):
                    split_layer_hi(l, B_OUT + SLOTS + i)
                split_xT_hi(3 * l + 2)
                load_norm(l, 2)
                ffn_group(l, 1, 0, B_FFN2, True, peeled=True)
                with act.Fori(1, NG - 1) as g:
                    ffn_group(l, 1, g, B_FFN2, True)
                ffn_group(l, 1, NG - 1, B_FFN2, False)

        @block.vector
        def _(dve):
            v = nc.vector

            def split_lo(n, s):
                dve.wait_ge(s_hi, n + 1)
                v.tensor_tensor(lo[:, s, :], raw[:, s, :], hi[:, s, :].bitcast(F32),
                                ALU.subtract).then_inc(s_lo, 1)

            def split_layer_lo(l, b):
                split_lo(BLOCKS * l + b, b % SLOTS)

            def lo_of_bank(c0, tt, bank):
                return v.tensor_tensor(xTl[:, c0:c0 + 4, P * tt:P * tt + P],
                                       bank[:, :].rearrange("p (c n) -> p c n", c=4),
                                       xTh[:, c0:c0 + 4, P * tt:P * tt + P].bitcast(F32), ALU.subtract)

            def split_xT_lo(r):
                for i in range(2 * TT):
                    dve.wait_ge(s_xh, 2 * TT * r + (i + 1))
                    lo_of_bank(4 * (i % 2), i // 2, B[i]).then_inc(s_xl, 1)

            def ffn_group(l, f, g, base, splits, peeled=False):
                it = (2 * NG) * l + (NG * f) + g
                for tt in range(TT):
                    dve.wait_ge(s_sil, TT * it + (tt + 1))
                    v.tensor_tensor(fh[:, tt, :], fsil[:, tt, :], B[tt][:, FG:2 * FG], ALU.mult).then_inc(s_h, 1)
                n0 = BLOCKS * l + base + SLOTS * g + SLOTS
                if splits:
                    split_lo(n0, 0)
                dve.wait_ge(s_hh, it + 1)
                v.tensor_tensor(hTl[:, 0:512], B[2][:, :], hTh[:, 0:512].bitcast(F32),
                                ALU.subtract).then_inc(s_hl, 1)
                if splits:
                    split_lo(n0 + 1, 1)
                    split_lo(n0 + 2, 2)

            def rsqrt(n, var, eps):
                a, y, t = vv[:, 0:n], rs[:, 0:n], rt[:, 0:n]
                v.tensor_scalar(a, var, eps, None, ALU.add)
                dve.drain()
                v.tensor_scalar(y.bitcast(I32), a.bitcast(I32), 1, None, ALU.logical_shift_right)
                dve.drain()
                v.tensor_scalar(y.bitcast(I32), y.bitcast(I32), -1.0, float(0x5F3759DF), ALU.mult, ALU.add)
                for _ in range(3):
                    dve.drain()
                    v.tensor_tensor(t, y, y, ALU.mult)
                    dve.drain()
                    v.scalar_tensor_tensor(t, t, -0.5, a, ALU.mult, ALU.mult)
                    dve.drain()
                    v.scalar_tensor_tensor(y, t, 1.5, y, ALU.add, ALU.mult)
                dve.drain()

            def layer_norm(l, q):
                r = 3 * l + q
                alpha, eps = (2 * ALPHA, 4 * EPS) if q != 1 else (ALPHA, EPS)
                for tt in range(TT):
                    if tt == 0:
                        dve.wait_ge(s_acc, r + 1)
                    else:
                        block_used(dve, l, (B_MIX, B_FFN2, BLOCKS)[q] - 1)
                    for hf in range(2):
                        v.scalar_tensor_tensor(U[:, tt, half_cols(hf)], X[:, tt, half_cols(hf)], alpha,
                                               B[4 + 2 * tt + hf][:, :], ALU.mult, ALU.add)
                    dve.drain()
                    for hf in range(2):
                        v.bn_stats(st[:, hf, :], U[:, tt, half_cols(hf)])
                    dve.drain()
                    v.bn_aggr(mv[:, 0, :], st[:, 0:2, :])
                    dve.drain()
                    rsqrt(1, mv[:, 0, 1:2], eps)
                    v.tensor_scalar(X[:, tt, :], U[:, tt, :], mv[:, 0, 0:1], rs[:, 0:1], ALU.subtract, ALU.mult)
                    dve.drain()
                    dve.wait_ge(s_pln, 16 * r + 16)
                    v.tensor_tensor(X[:, tt, :], X[:, tt, :], pln[:, 0:D], ALU.mult)
                    dve.drain()
                    v.tensor_tensor(X[:, tt, :], X[:, tt, :], pln[:, D:2 * D], ALU.add).then_inc(s_x, 1)

            def head_norm(srcs, dsts):
                n = len(srcs)
                for i, s in enumerate(srcs):
                    v.bn_stats(st[:, i, :], s)
                dve.drain()
                for i in range(n):
                    v.bn_aggr(mv[:, i, :], st[:, i:i + 1, :])
                dve.drain()
                rsqrt(n, mv[:, 0:n, 1], EPS)
                for i in range(n):
                    last = v.tensor_scalar(dsts[i], srcs[i], mv[:, i, 0:1], rs[:, i:i + 1],
                                           ALU.subtract, ALU.mult)
                return last

            v.memset(mprev[:, 0:1], 0.0)
            v.memset(ones4, 1.0)
            v.memset(mv1[:, :, :, ME:ME + 1], 1.0)
            dve.wait_ge(s_x_in, 16)
            for tt in range(TT):
                v.memset(dmax[:, tt:tt + 1], 0.0).then_inc(s_x, 1)
            dve.wait_ge(s_cst, 16)

            with dve.Fori(0, LAYERS) as l:
                for b in range(SLOTS):
                    split_layer_lo(l, b)
                split_xT_lo(3 * l)
                ffn_group(l, 0, 0, 0, True, peeled=True)
                with dve.Fori(1, NG) as g:
                    ffn_group(l, 0, g, 0, True)
                layer_norm(l, 0)
                split_xT_lo(3 * l + 1)

                dve.wait_ge(s_small_hi, l + 1)
                v.tensor_tensor(hTl[:, :], wsm_raw, hTh[:, :].bitcast(F32), ALU.subtract).then_inc(s_small_lo, 1)
                dve.wait_ge(s_small_ps, l + 1)
                v.tensor_copy(aT, B[4][0:RANK, 0:SEQ]).then_inc(s_small_out, 1)
                v.tensor_copy(G_, B[4][32:32 + MH, 0:SEQ])
                v.tensor_copy(gf, B[4][64:64 + MH, 0:SEQ])
                v.memset(attm, 0.0)
                v.memset(cin[:, :, 0:CONV - 1], 0.0)
                dve.drain()
                v.tensor_scalar(G_, G_, bif_t[:, 0:1], None, ALU.add)
                v.tensor_scalar(gf, gf, bif_t[:, 1:2], None, ALU.add)
                for k in range(2 * NGRP):
                    if k % 2 and k // 2 >= G_GATE:
                        i = k // 2
                        j = i - G_GATE
                        dve.wait_ge(s_bg[j % 2], 48 * l + (16 * (j // 2) + 16))
                        for tt in range(TT):
                            group_tile_done(dve, l, i, tt)
                            last = v.tensor_tensor(gates[:, tt, 512 * j:512 * j + 512], B[2 * (i % 2) + tt][:, :],
                                                   bg[:, j % 2, :], ALU.add)
                        last.then_inc(s_gates_out, 1)
                    if k == 1:
                        dve.wait_ge(s_gla_gate_ps, l + 1)
                        v.tensor_tensor(la.rearrange("p (t n) -> p t n", t=TT),
                                        B[5][:, :].rearrange("p (t n) -> p t n", t=TT),
                                        vec[:, V_BA:V_BA + 256].unsqueeze(1).to_broadcast([P, TT, 256]), ALU.add)
                        dve.drain()
                        v.scalar_tensor_tensor(le, la, -1.0, la, ALU.mult, ALU.max)
                        v.scalar_tensor_tensor(EM, gf, -1.0, gf, ALU.mult, ALU.max).then_inc(s_gate_abs, 1)
                        dve.wait_ge(s_softplus, l + 1)
                        v.scalar_tensor_tensor(la, la, 0.0, le, ALU.min, ALU.subtract).then_inc(s_log_sig, 1)
                        v.scalar_tensor_tensor(gf, gf, 0.0, EM, ALU.min, ALU.subtract)
                        dve.drain()
                        for c in range(NC):
                            cs = slice(LC * c, LC * c + LC)
                            v.tensor_tensor_scan(F_[:, cs], ones4, gf[:, cs], 0.0, ALU.mult, ALU.add)
                        dve.drain()
                        v.tensor_tensor(G_, G_, F_, ALU.subtract)
                        dve.drain()
                        for c in range(NC):
                            cs = slice(LC * c, LC * c + LC)
                            end = LC * c + LC - 1
                            v.tensor_tensor_scan(M_[:, cs], G_[:, cs], G_[:, cs], mprev[:, c:c + 1],
                                                 ALU.max, ALU.max)
                            dve.drain()
                            v.tensor_tensor(mprev[:, c + 1:c + 2], F_[:, end:end + 1], M_[:, end:end + 1], ALU.add)
                            v.tensor_scalar(WI[:, cs], M_[:, cs], mprev[:, c:c + 1], None, ALU.subtract)
                            v.tensor_scalar(WK[:, cs], G_[:, cs], M_[:, end:end + 1], None, ALU.subtract)
                            dve.drain()
                        v.tensor_tensor(EM, F_, M_, ALU.add).then_inc(s_ml_rows, 1)
                    if k == 4:
                        dve.wait_ge(s_gla_decay, l + 1)
                        v.scalar_tensor_tensor(qdT, B[6][:, :], GK ** -0.5, E1, ALU.mult, ALU.mult)
                        v.tensor_tensor(kiT, B[7][:, :], E2, ALU.mult)
                        v.tensor_tensor(kd.rearrange("p (t n) -> p t n", t=TT), T0[:, :, 256:512],
                                                   E3.rearrange("p (t n) -> p t n", t=TT), ALU.mult).then_inc(s_gla_qk, 1)
                    if k == 7:
                        dve.wait_ge(s_gla_scores, l + 1)
                        v.tensor_copy(gst[:, 0, :, :], B[6][:, 0:256].rearrange("p (a n) -> p a n", a=2))
                        for q in range(2):
                            last = v.copy_predicated(attm[:, q, :].rearrange("p (h n) -> p h n", h=GH),
                                                     tri.bitcast(I32).unsqueeze(1).to_broadcast([P, GH, P]),
                                                     B[4 + q][:, :].rearrange("p (h n) -> p h n", h=GH))
                        for c in (1, 2):
                            dve.drain()
                            for a in range(2):
                                kv = B[6 + c % 2][:, 256 * (c // 2) + P * a:256 * (c // 2) + P * a + P]
                                end = SEQ * a + LC * c + LC - 1
                                last = v.scalar_tensor_tensor(gst[:, c, a, :], gst[:, c - 1, a, :],
                                                              E1[:, end:end + 1], kv, ALU.mult, ALU.add)
                        last.then_inc(s_gla_state, 1)
                    if k == 9:
                        dve.wait_ge(s_gla_out, l + 1)
                        tiles = [(tt, h) for tt in range(TT) for h in range(GH)]
                        head_norm([B[4 + h % 2][:, 256 * tt + P * (h // 2):256 * tt + P * (h // 2) + P]
                                              for tt, h in tiles],
                                             [gyn[:, tt, P * h:P * h + P] for tt, h in tiles]).then_inc(s_gla_norm, 1)
                        dve.drain()
                        v.tensor_tensor(gyn, gyn, vec[:, V_GG:V_GG + 512].unsqueeze(1).to_broadcast([P, TT, 512]),
                                        ALU.mult)
                        dve.drain()
                        dve.wait_ge(s_group_out, G_GATE * l + (G_GR + 1))
                        v.tensor_tensor(gr[:, :, :], gyn, gr[:, :, :], ALU.mult)
                    h = k - 12
                    if 0 <= h < DH:
                        v.scalar_tensor_tensor(bh[:, :], cst[:, C_DIST:C_DIST + 384], -(2.0 ** -(h + 1)),
                                               cst[:, C_LNC:C_LNC + 384], ALU.mult, ALU.add)
                        dve.drain()
                        dve.wait_ge(s_dil_scores, DH * l + (h + 1))
                        v.scalar_tensor_tensor(dL, B[4][:, 0:384], DE ** -0.5, bh[:, :], ALU.mult, ALU.add)
                        dve.drain()
                        v.tensor_reduce(dmax[:, 0:1], dL[:, 0:P], AX, ALU.max, negate=True)
                        v.tensor_reduce(dmax[:, 1:2], dL[:, P:3 * P], AX, ALU.max, negate=True).then_inc(s_dil_logits, 1)
                    if k == 22:
                        dve.wait_ge(s_dil_exp, DH * l + DH)
                        v.reciprocal(drec, dsum)
                        dve.drain()
                        dve.wait_ge(s_dil_pv, DH * l + DH)
                        dve.wait_ge(s_ml_q_T, l + 1)
                        for tt in range(TT):
                            last = v.tensor_tensor(T1[:, tt, :].rearrange("p (h n) -> p h n", h=DH),
                                                   B[6 + tt][:, :].rearrange("p (h n) -> p h n", h=DH),
                                                   drec[:, tt, :].unsqueeze(2).to_broadcast([P, DH, DE]), ALU.mult)
                        last.then_inc(s_dil_y, 1)
                    if k == 23:
                        dve.wait_ge(s_ml_cols, l + 1)
                        v.tensor_copy(mc.rearrange("p t q h -> p (t q h)"), B[6][:, 0:32])
                        v.tensor_copy(ac.rearrange("p h c -> p (h c)"), B[7][:, 0:16]).then_inc(s_ml_mc, 1)
                    if k in (24, 25):
                        j0 = 0 if k == 24 else MH
                        dve.wait_ge(s_conv_in, 2 * l + (1 if k == 24 else 2))
                        for i in range(CONV):
                            for j in range(MH):
                                src, dst, w = cin[:, j, i:i + SEQ], qkT[:, j0 + j, :], cvp[:, j0 + j, :]
                                if i == 0:
                                    last = v.tensor_scalar(dst, src, w[:, 0:1], w[:, CONV:CONV + 1],
                                                           ALU.mult, ALU.add)
                                else:
                                    last = v.scalar_tensor_tensor(dst, src, w[:, i:i + 1], dst, ALU.mult, ALU.add)
                            if i < CONV - 1:
                                dve.drain()
                        last.then_inc(s_conv, 1)
                    if k == 27:
                        dve.wait_ge(s_ml_scores, l + 1)
                        for tt in range(TT):
                            last = v.scalar_tensor_tensor(mA[:, tt, :], B[4 + tt][:, :], ME ** -0.5, mA[:, tt, :],
                                                          ALU.mult, ALU.mult)
                        last.then_inc(s_ml_A, 1)
                        dve.wait_ge(s_ml_k_nat, l + 1)
                        for tt in range(TT):
                            for hh in range(MH):
                                last = v.tensor_scalar(mkw[:, tt, P * hh:P * hh + P], B[6 + tt][:, P * hh:P * hh + P],
                                                       mc[:, tt, 2, hh:hh + 1], ME ** -0.5, ALU.mult, ALU.mult)
                    if k == 28:
                        dve.wait_ge(s_ml_inter_b, l + 1)
                        for i in range(2):
                            last = v.tensor_tensor(qwT[:, 2 * i:2 * i + 2, :], qkT[:, 2 * i:2 * i + 2, :],
                                                   B[4 + i][:, :].rearrange("p (h n) -> p h n", h=2), ALU.mult)
                        last.then_inc(s_ml_q, 1)
                    if k in (29, 30):
                        h0 = 0 if k == 29 else 2
                        dve.wait_ge(s_ml_kv, 2 * l + (1 if k == 29 else 2))
                        for c in range(NC - 1):
                            for hh in range(2):
                                kv = B[(6, 7, 4)[c]][:, (ME + 1) * hh:(ME + 1) * (hh + 1)]
                                if c == 0:
                                    last = v.tensor_copy(mcs[:, 0, h0 + hh, :], kv)
                                else:
                                    last = v.scalar_tensor_tensor(mcs[:, c, h0 + hh, :], mcs[:, c - 1, h0 + hh, :],
                                                                  ac[:, h0 + hh, c:c + 1], kv, ALU.mult, ALU.add)
                            if c < NC - 2:
                                dve.drain()
                        last.then_inc(s_ml_state, 1)
                    split_layer_lo(l, B_MIX + k + SLOTS)

                def split_y_lo(copied, split, n, i, b0, c0):
                    dve.wait_ge(copied, n * l + (i + 1))
                    for tt in range(TT):
                        last = lo_of_bank(c0, tt, B[b0 + tt])
                    last.then_inc(split, 1)

                def gate_branch(b, j):
                    block_used(dve, l, B_PROJ + 2 * b + j)
                    dve.wait_ge(s_gate_sig, 3 * l + (b + 1))
                    cols = slice(D * b + 512 * j, D * b + 512 * j + 512)
                    mcol = slice(512 * j, 512 * j + 512)
                    for tt in range(TT):
                        last = v.tensor_tensor(gates[:, tt, cols], gates[:, tt, cols], B[2 * j + tt][:, :], ALU.mult)
                    if b:
                        dve.drain()
                        last = v.tensor_tensor(gates[:, :, mcol], gates[:, :, mcol], gates[:, :, cols], ALU.add)
                    last.then_inc(s_merged, 1)

                split_y_lo(s_y_hi, s_y_lo, 3, 0, 0, 0)
                split_y_lo(s_y_hi, s_y_lo, 3, 1, 2, 4)
                split_layer_lo(l, B_PROJ + SLOTS)
                for tt in range(TT):
                    for a in range(2):
                        ps = B[4 + 2 * tt + a][:, 0:2 * (ME + 1)].rearrange("p (h n) -> p h n", h=2)
                        dve.drain()
                        dve.wait_ge(s_ml_out, TT * l + (tt + 1))
                        den = ps[:, :, ME:ME + 1]
                        v.scalar_tensor_tensor(rden.unsqueeze(2), den, -1.0,
                                               mc[:, tt, 3, 2 * a:2 * a + 2].unsqueeze(2), ALU.mult, ALU.max)
                        dve.drain()
                        v.tensor_tensor(rden.unsqueeze(2), den, rden.unsqueeze(2), ALU.max)
                        dve.drain()
                        v.reciprocal(rden, rden)
                        dve.drain()
                        v.tensor_tensor(mkw[:, tt, 256 * a:256 * a + 256].rearrange("p (h n) -> p h n", h=2),
                                        ps[:, :, 0:ME], rden.unsqueeze(2).to_broadcast([P, 2, ME]), ALU.mult)
                dve.drain()
                tiles = [mkw[:, tt, P * h:P * h + P] for tt in range(TT) for h in range(MH)]
                head_norm(tiles, tiles)
                dve.drain()
                v.tensor_tensor(mkw, mkw, vec[:, V_MG:V_MG + 512].unsqueeze(1).to_broadcast([P, TT, 512]), ALU.mult)
                dve.drain()
                dve.wait_ge(s_out_gate, l + 1)
                v.tensor_tensor(mo[:, :, :], mkw, mo[:, :, :], ALU.mult).then_inc(s_ml_y, 1)
                gate_branch(0, 0)
                split_layer_lo(l, B_PROJ + SLOTS + 1)
                gate_branch(0, 1)
                split_layer_lo(l, B_PROJ + SLOTS + 2)
                gate_branch(1, 0)
                split_layer_lo(l, B_PROJ + SLOTS + 3)
                gate_branch(1, 1)
                split_y_lo(s_y_hi, s_y_lo, 3, 2, 4, 0)
                split_layer_lo(l, B_PROJ + SLOTS + 4)
                gate_branch(2, 0)
                split_layer_lo(l, B_PROJ + SLOTS + 5)
                gate_branch(2, 1)
                split_y_lo(s_merged_hi, s_merged_lo, 2, 0, 0, 0)
                split_y_lo(s_merged_hi, s_merged_lo, 2, 1, 2, 4)
                for i in range(4):
                    split_layer_lo(l, B_OUT + SLOTS + i)
                layer_norm(l, 1)
                split_xT_lo(3 * l + 2)
                ffn_group(l, 1, 0, B_FFN2, True, peeled=True)
                with dve.Fori(1, NG - 1) as g:
                    ffn_group(l, 1, g, B_FFN2, True)
                ffn_group(l, 1, NG - 1, B_FFN2, False)
                layer_norm(l, 2)

        @block.tensor
        def _(pe):
            def mm(*a, start=True, stop=True):
                return nc.tensor.matmul(*a, start=start, stop=stop, skip_group_check=True)

            def mm3(ps, ah, al, wh, wl, start, stop):
                mm(ps, ah, wh, start=start, stop=False)
                mm(ps, ah, wl, start=False, stop=False)
                return mm(ps, al, wh, start=False, stop=stop)

            def wide_block(n, s, psums, c0, first, last, signal=None):
                pe.wait_ge(s_lo, n + 1)
                for tt in range(TT):
                    for c in range(4):
                        w = slice(512 * c, 512 * c + 512)
                        tok = slice(P * tt, P * tt + P)
                        ins = mm3(psums[tt], xTh[:, c0 + c, tok], xTl[:, c0 + c, tok], hi[:, s, w], lo[:, s, w],
                                  first and c == 0, last and c == 3)
                    if signal and tt == 0:
                        signal(ins)
                ins.then_inc(s_used, 1)

            def layer_block(l, b, psums, c0, first, last, signal=None):
                wide_block(BLOCKS * l + b, b % SLOTS, psums, c0, first, last, signal)

            def transpose_x(r):
                for tt in range(TT):
                    pe.wait_ge(s_x, TT * r + (tt + 1))
                    for hf in range(2):
                        for c in range(4):
                            last = nc.tensor.transpose(B[2 * tt + hf][:, P * c:P * c + P],
                                                       X[:, tt, 512 * hf + P * c:512 * hf + P * c + P], ident)
                        last.then_inc(s_xt, 1)
                pe.wait_ge(s_xl, 2 * TT * r + 2 * TT)

            def gate_up(n, s0, s1):
                wide_block(n, s0, (B[0][:, :], B[1][:, :]), 0, True, False)
                wide_block(n + 1, s1, (B[0][:, :], B[1][:, :]), 4, False, True,
                           lambda ins: ins.then_inc(s_gu, 1))

            def transpose_h(it):
                pe.wait_ge(s_h, TT * it + TT)
                for c in range(2):
                    for tt in range(TT):
                        last = nc.tensor.transpose(B[2][:, SEQ * c + P * tt:SEQ * c + P * tt + P],
                                                   fh[:, tt, P * c:P * c + P], ident)
                last.then_inc(s_ht, 1)

            def down(it, n, s, first, last):
                pe.wait_ge(s_lo, n + 1)
                pe.wait_ge(s_hl, it + 1)
                for tt in range(TT):
                    for hf in range(2):
                        for c in range(2):
                            a = slice(SEQ * c + P * tt, SEQ * c + P * tt + P)
                            w = slice(D * c + 512 * hf, D * c + 512 * hf + 512)
                            ins = mm3(B[4 + 2 * tt + hf][:, :], hTh[:, a], hTl[:, a], hi[:, s, w], lo[:, s, w],
                                      first and c == 0, last and c == 1)
                    if last and tt == 0:
                        ins.then_inc(s_acc, 1)
                ins.then_inc(s_used, 1)

            def ffn(l, f, base):
                it0 = (2 * NG) * l + (NG * f)
                n0 = BLOCKS * l + base
                gate_up(n0, 0, 1)
                transpose_h(it0)
                gate_up(n0 + 2, 2, 0)
                down(it0, n0 + 4, 1, True, False)
                transpose_h(it0 + 1)
                with pe.Fori(2, NG) as g:
                    gate_up(n0 + SLOTS * g - 1, 2, 0)
                    down(it0 + g - 1, n0 + SLOTS * g + 1, 1, False, False)
                    transpose_h(it0 + g)
                down(it0 + (NG - 1), n0 + (FB - 1), 2, False, True)

            def four_transposes(bank, src):
                for c in range(4):
                    last = nc.tensor.transpose(bank[:, P * c:P * c + P], src[:, P * c:P * c + P], ident)
                return last

            for _ in range(SLOTS):
                pe.nop().then_inc(s_used, 1)
            pe.wait_ge(s_cst, 16)
            with pe.Fori(0, LAYERS) as l:
                transpose_x(3 * l)
                ffn(l, 0, 0)
                transpose_x(3 * l + 1)

                pe.wait_ge(s_small_lo, l + 1)
                for c in range(KD):
                    a = slice(SM * c, SM * c + SM)
                    last = mm3(B[4][0:SM, 0:SEQ], hTh[:, a], hTl[:, a], xTh[:, c, :], xTl[:, c, :],
                               c == 0, c == KD - 1)
                last.then_inc(s_small_ps, 1)
                for k in range(2 * NGRP):
                    i = k // 2
                    if k % 2 == 0 and i >= 2:
                        if i - 2 < G_GATE:
                            pe.wait_ge(s_group_out, G_GATE * l + (i - 1))
                        else:
                            pe.wait_ge(s_gates_out, GATE_GRPS * l + (i - 1 - G_GATE))
                    layer_block(l, B_MIX + k, (B[2 * (i % 2)][:, :], B[2 * (i % 2) + 1][:, :]), 4 * (k % 2),
                                k % 2 == 0, k % 2 == 1,
                                (lambda ins: ins.then_inc(s_group0, 1)) if k % 2 else None)
                    if k == 1:
                        pe.wait_ge(s_small_out, l + 1)
                        for tt in range(TT):
                            last = mm(B[5][:, 256 * tt:256 * tt + 256], aT[:, P * tt:P * tt + P], wa2_t)
                        last.then_inc(s_gla_gate_ps, 1)
                    if k == 3:
                        pe.wait_ge(s_group_out, G_GATE * l + (G_GQK + 1))
                        for q in range(2):
                            for a in range(2):
                                for tt in range(TT):
                                    last = nc.tensor.transpose(
                                        B[6 + q][:, SEQ * a + P * tt:SEQ * a + P * tt + P],
                                        T0[:, tt, 256 * q + P * a:256 * q + P * a + P], ident)
                    if k == 4:
                        pe.wait_ge(s_log_sig, l + 1)
                        for a in range(2):
                            for tt in range(TT):
                                mm(B[4][:, SEQ * a + P * tt:SEQ * a + P * tt + P],
                                   la[:, 256 * tt + P * a:256 * tt + P * a + P], tri)
                        for tt in range(TT):
                            last = mm(B[5][:, 256 * tt:256 * tt + 256], cst[:, C_SUF:C_SUF + P],
                                      la[:, 256 * tt:256 * tt + 256])
                        last.then_inc(s_gla_cum, 1)
                    if k == 7:
                        pe.wait_ge(s_gla_qk, l + 1)
                        pe.wait_ge(s_group_out, G_GATE * l + (G_GV + 1))
                        for tt in range(TT):
                            for h in range(GH):
                                r0, c0 = GK * (h % 2), SEQ * (h // 2) + P * tt
                                col = 256 * tt + P * (h // 2)
                                last = mm(B[4 + h % 2][:, col:col + P], kiT[r0:r0 + GK, c0:c0 + P],
                                          qdT[r0:r0 + GK, c0:c0 + P])
                        for c in range(NC - 1):
                            tt, r0 = c // 2, LC * (c % 2)
                            for h in range(GH):
                                o0, col = GK * (h % 2), 256 * (c // 2) + P * (h // 2)
                                last = mm(B[6 + c % 2][o0:o0 + GK, col:col + P],
                                          kd[r0:r0 + LC, 256 * tt + GK * h:256 * tt + GK * h + GK],
                                          gv[r0:r0 + LC, tt, GV * h:GV * h + GV])
                        last.then_inc(s_gla_scores, 1)
                    if k == 9:
                        pe.wait_ge(s_gla_state, l + 1)
                        for tt in range(TT):
                            for h in range(GH):
                                col = 256 * tt + P * (h // 2)
                                ps = B[4 + h % 2][:, col:col + P]
                                last = mm(ps, attm[:, h % 2, col:col + P], gv[:, tt, P * h:P * h + P], stop=False)
                                for c in (2 * tt, 2 * tt + 1):
                                    if c:
                                        r0, o0 = GK * (h % 2), LC * (c % 2)
                                        q0 = SEQ * (h // 2) + LC * c
                                        last = mm(B[4 + h % 2][o0:o0 + LC, col:col + P],
                                                  qdT[r0:r0 + GK, q0:q0 + LC],
                                                  gst[r0:r0 + GK, c - 1, h // 2, :], start=False)
                        last.then_inc(s_gla_out, 1)
                    if k in (10, 11):
                        src, b0, g = (T1, 6, G_DQ) if k == 10 else (T0, 4, G_DK)
                        pe.wait_ge(s_group_out, G_GATE * l + (g + 1))
                        pe.wait_ge(s_gla_state if k == 10 else s_gla_norm, l + 1)
                        for tt in range(TT):
                            last = four_transposes(B[b0 + tt], src[:, tt, :])
                        last.then_inc(s_dil_q_T if k == 10 else s_dil_k_T, 1)
                    h = k - 12
                    if 0 <= h - 2 < DH:
                        g = h - 2
                        pe.wait_ge(s_dil_pT, DH * l + (g + 1))
                        if g == 0:
                            pe.wait_ge(s_group_out, G_GATE * l + (G_DV + 1))
                        cols = slice(DE * g, DE * g + DE)
                        mm(B[6][:, cols], dPT[:, 0:P], dv[:, 0, cols])
                        mm(B[7][:, cols], dPT[:, P:2 * P], dv[:, 0, cols], stop=False)
                        mm(B[7][:, cols], dPT[:, 2 * P:3 * P], dv[:, 1, cols], start=False).then_inc(s_dil_pv, 1)
                    if 0 <= h - 1 < DH:
                        pe.wait_ge(s_dil_exp, DH * l + h)
                        for i3 in range(3):
                            last = nc.tensor.transpose(B[5][:, P * i3:P * i3 + P], dL[:, P * i3:P * i3 + P], ident)
                        last.then_inc(s_dil_p_T, 1)
                    if 0 <= h < DH:
                        if h == 0:
                            pe.wait_ge(s_dil_kT, l + 1)
                        r0, a = DE * (h % 2), h // 2
                        mm(B[4][:, 0:P], dqT[r0:r0 + DE, a, 0:P], dkT[r0:r0 + DE, a, 0:P])
                        mm(B[4][:, P:3 * P], dqT[r0:r0 + DE, a, P:2 * P], dkT[r0:r0 + DE, a, :]).then_inc(s_dil_scores, 1)
                    if k in (22, 24):
                        src, g = (T1, G_MQ) if k == 22 else (T0, G_MK)
                        if k == 22:
                            pe.wait_ge(s_group_out, G_GATE * l + (g + 1))
                        else:
                            pe.wait_ge(s_conv_in, 2 * l + 1)
                        if k == 22:
                            pe.wait_ge(s_dil_pT, DH * l + DH)
                        for tt in range(TT):
                            last = four_transposes(B[4 + tt], src[:, tt, :])
                        last.then_inc(s_ml_q_T if k == 22 else s_ml_k_T, 1)
                    if k == 23:
                        pe.wait_ge(s_dil_y, l + 1)
                        pe.wait_ge(s_ml_rows_exp, l + 1)
                        for hh in range(MH):
                            last = mm(B[7][:, 4 * hh:4 * hh + NC], cst[0:MH, C_SEL + P * hh:C_SEL + P * hh + P],
                                      WI[:, LC - 1:SEQ:LC])
                        for tt in range(TT):
                            for q, row in enumerate((G_, WI, WK, EM)):
                                col = 4 * (4 * tt + q)
                                last = nc.tensor.transpose(B[6][:, col:col + MH], row[:, P * tt:P * tt + P],
                                                           ident[0:MH, 0:MH])
                        last.then_inc(s_ml_cols, 1)
                    if k == 25:
                        pe.wait_ge(s_conv_in, 2 * l + 2)
                        for tt in range(TT):
                            for hh in range(MH):
                                ps = B[4 + tt][:, P * hh:P * hh + P]
                                mm(ps, cst[0:MH, C_SEL + P * hh:C_SEL + P * hh + P], M_[:, P * tt:P * tt + P], stop=False)
                                last = mm(ps, ident, cst[:, C_BIG:C_BIG + P], start=False)
                        last.then_inc(s_ml_max_b, 1)
                    if k == 27:
                        pe.wait_ge(s_ml_weights, l + 1)
                        for tt in range(TT):
                            tok = slice(P * tt, P * tt + P)
                            for hh in range(MH):
                                last = mm(B[4 + tt][:, P * hh:P * hh + P], qkT[:, MH + hh, tok], qkT[:, hh, tok])
                        last.then_inc(s_ml_scores, 1)
                        pe.wait_ge(s_ml_mc, l + 1)
                        for tt in range(TT):
                            for hh in range(MH):
                                last = nc.tensor.transpose(B[6 + tt][:, P * hh:P * hh + P],
                                                           qkT[:, MH + hh, P * tt:P * tt + P], ident)
                        last.then_inc(s_ml_k_nat, 1)
                    if k == 28:
                        pe.wait_ge(s_ml_A, l + 1)
                        for hh in range(MH):
                            last = mm(B[4 + hh // 2][:, SEQ * (hh % 2):SEQ * (hh % 2) + SEQ],
                                      cst[0:MH, C_SEL + P * hh:C_SEL + P * hh + P], WI)
                        last.then_inc(s_ml_inter_b, 1)
                    if k in (29, 30):
                        h0 = 0 if k == 29 else 2
                        if k == 29:
                            pe.wait_ge(s_ml_q, l + 1)
                        else:
                            pe.wait_ge(s_ml_state, 2 * l + 1)
                        for hh in range(2):
                            for c in range(NC - 1):
                                tt, r0 = c // 2, LC * (c % 2)
                                last = mm(B[(6, 7, 4)[c]][:, (ME + 1) * hh:(ME + 1) * (hh + 1)],
                                          mkw[r0:r0 + LC, tt, P * (h0 + hh):P * (h0 + hh) + P],
                                          mv1[r0:r0 + LC, tt, h0 + hh, :])
                        last.then_inc(s_ml_kv, 1)

                pe.wait_ge(s_gates_out, GATE_GRPS * l + (GATE_GRPS - 1))
                for tt in range(TT):
                    last = four_transposes(B[tt], gr[:, tt, :])
                last.then_inc(s_yT, 1)
                pe.wait_ge(s_gates_out, GATE_GRPS * l + GATE_GRPS)
                for tt in range(TT):
                    last = four_transposes(B[2 + tt], T1[:, tt, :])
                last.then_inc(s_yT, 1)
                pe.wait_ge(s_ml_state, 2 * l + 2)
                for tt in range(TT):
                    for hh in range(MH):
                        col = (ME + 1) * (hh % 2)
                        bank = B[4 + 2 * tt + hh // 2]
                        last = mm(bank[:, col:col + ME + 1], mA[:, tt, P * hh:P * hh + P], mv1[:, tt, hh, :], stop=False)
                        for c in (2 * tt, 2 * tt + 1):
                            if c:
                                o0 = LC * (c % 2)
                                last = mm(bank[o0:o0 + LC, col:col + ME + 1], qwT[:, hh, LC * c:LC * c + LC],
                                          mcs[:, c - 1, hh, :], start=False)
                    last.then_inc(s_ml_out, 1)

                def project(b, j, c0):
                    layer_block(l, B_PROJ + 2 * b + j, (B[2 * j][:, :], B[2 * j + 1][:, :]), c0, True, True)

                pe.wait_ge(s_y_lo, 3 * l + 2)
                project(0, 0, 0)
                project(0, 1, 0)
                for j in range(2):
                    pe.wait_ge(s_merged, 6 * l + (j + 1))
                    project(1, j, 4)
                pe.wait_ge(s_ml_y, l + 1)
                for tt in range(TT):
                    last = four_transposes(B[4 + tt], mo[:, tt, :])
                last.then_inc(s_yT, 1)
                pe.wait_ge(s_y_lo, 3 * l + 3)
                for j in range(2):
                    pe.wait_ge(s_merged, 6 * l + (j + 3))
                    project(2, j, 0)
                for j in range(2):
                    pe.wait_ge(s_merged, 6 * l + (j + 5))
                    for tt in range(TT):
                        last = four_transposes(B[2 * j + tt], gates[:, tt, 512 * j:512 * j + 512])
                    last.then_inc(s_merged_T, 1)
                for c in range(2):
                    pe.wait_ge(s_merged_lo, 2 * l + (c + 1))
                    for j in range(2):
                        layer_block(l, B_OUT + 2 * c + j, (B[4 + j][:, :], B[6 + j][:, :]), 4 * c, c == 0, c == 1,
                                    (lambda ins: ins.then_inc(s_acc, 1)) if c and j else None)
                transpose_x(3 * l + 2)
                ffn(l, 1, B_FFN2)


def shape_constants():
    c = np.zeros((P, C_W), np.float32)
    s, t = np.arange(P)[:, None], np.arange(P)[None, :]
    same = s // LC == t // LC
    c[:, C_ID:C_ID + P] = s == t
    c[:, C_TRI:C_TRI + P] = same & (s <= t)
    c[:, C_SUF:C_SUF + P] = same & (s > t)
    c[:, C_BIG:C_BIG + P] = np.where(same & (s <= t), 0.0, BIG)
    q = np.arange(P)[:, None]
    dist = np.concatenate([q - t, q + P - np.arange(SEQ)[None, :]], axis=1)
    count = sum(((dist % dil == 0) & (dist <= window)).astype(int) for window, dil in
                ((128, 1), (512, 4), (2048, 16)))
    count = np.where(dist >= 0, count, 0)
    c[:, C_DIST:C_DIST + 384] = dist
    c[:, C_LNC:C_LNC + 384] = np.where(count > 0, np.log(np.maximum(count, 1)), -BIG)
    for h in range(MH):
        c[h, C_SEL + P * h:C_SEL + P * h + P] = 1.0
    return c


def weight_stream(inputs):
    s = np.empty((LAYERS, BLOCKS, P, BW), np.float32)

    def wide(w, c0, cols):
        return w[P * c0:P * c0 + 4 * P, cols].reshape(4, P, 512).transpose(1, 0, 2).reshape(P, BW)

    def down(w, g):
        return w[2 * P * g:2 * P * g + 2 * P].reshape(2, P, D).transpose(1, 0, 2).reshape(P, BW)

    widths = (256, 256, 512, 512, 16, 512, 512, 512, 512, 512, 512, 4, 4, 512, 3 * D)
    at = [0]
    for w in widths:
        at.append(at[-1] + w)
    gq, _, gv, gr, _, dq, dk, dv, mq, mk, mv, _, _, mo, gates, _ = at
    groups = [gq, gv, gr, dq, dk, dv, mq, mk, mv, mo] + [gates + 512 * i for i in range(6)]
    for l in range(LAYERS):
        for f, base in ((1, 0), (2, B_FFN2)):
            wg, wu, wd = (np.asarray(inputs[f"ffn{f}_w_{n}"])[l] for n in ("gate", "up", "down"))
            for g in range(NG):
                gu = np.concatenate([wg[:, FG * g:FG * g + FG], wu[:, FG * g:FG * g + FG]], axis=1)
                n = base if g == 0 else base + SLOTS * g - 1
                s[l, n], s[l, n + 1] = wide(gu, 0, slice(0, 512)), wide(gu, 4, slice(0, 512))
                s[l, base + SLOTS * g + 4 if g < NG - 1 else base + FB - 1] = down(wd, g)
        w = np.asarray(inputs["w_in"])[l]
        for i, c in enumerate(groups):
            for k in range(2):
                s[l, B_MIX + 2 * i + k] = wide(w, 4 * k, slice(c, c + 512))
        for b, n in enumerate(("gla", "dil", "ml")):
            w = np.asarray(inputs[f"w_proj_{n}"])[l]
            for j in range(2):
                s[l, B_PROJ + 2 * b + j] = wide(w, 0, slice(512 * j, 512 * j + 512))
        w = np.asarray(inputs["w_out"])[l]
        for c in range(2):
            for j in range(2):
                s[l, B_OUT + 2 * c + j] = wide(w, 4 * c, slice(512 * j, 512 * j + 512))
    return s.reshape(LAYERS * BLOCKS, P, BW)


def kernel(**inputs):
    import concourse.bacc as _bacc
    from concourse.bass_utils import run_bass_kernel_spmd as _run

    a = {n: np.asarray(v) for n, v in inputs.items()}
    w_in = a["w_in"].reshape(LAYERS, KD, P, -1)
    wsmall = np.zeros((LAYERS, P, KD, SM), np.float32)
    wsmall[..., 0:16] = w_in[..., 1536:1552].transpose(0, 2, 1, 3)
    wsmall[..., 32:36] = w_in[..., 4624:4628].transpose(0, 2, 1, 3)
    wsmall[..., 64:68] = w_in[..., 4628:4632].transpose(0, 2, 1, 3)
    conv = np.concatenate([a["ml_conv_w"], a["ml_conv_b"][:, None, :]], axis=1)
    arrays = {
        "x": a["x"].reshape(SEQ, D),
        "stream": weight_stream(inputs),
        "consts": shape_constants(),
        "lnp": np.stack([np.concatenate([a[f"ln{i}_g"], a[f"ln{i}_b"]], axis=1) for i in (1, 2, 3)], axis=1),
        "vecs": np.concatenate([a["gla_norm_g"], a["ml_norm_g"], a["gla_b_a"]], axis=1),
        "bgate": a["b_gate"],
        "wsmall": wsmall.reshape(LAYERS, P, KD * SM),
        "wa2": a["gla_w_a2"],
        "bif": np.stack([a["ml_b_i"], a["ml_b_f"]], axis=2),
        "convp": conv.reshape(LAYERS, CONV + 1, 2 * MH, P).transpose(0, 3, 2, 1),
    }
    arrays = {n: np.ascontiguousarray(v) for n, v in arrays.items()}
    nc = _bacc.Bacc("TRN2", target_bir_lowering=False, num_devices=1)
    args = [nc.dram_tensor(n, v.shape, F32, kind="ExternalInput").ap() for n, v in arrays.items()]
    out = nc.dram_tensor("out", (SEQ, D), F32, kind="ExternalOutput").ap()
    trunk(nc, *args, out)
    r = _run(nc, [arrays], core_ids=[0])
    return r.results[0]["out"].reshape(1, SEQ, D)
```

```python
from contextlib import ExitStack

import numpy as np

import concourse.bass as bass
from concourse import mybir

ALU = mybir.AluOpType
ACT = mybir.ActivationFunctionType
F32 = mybir.dt.float32
F32R = mybir.dt.float32r
I32 = mybir.dt.int32
AX = mybir.AxisListType.X

P = 128
LAYERS, SEQ, D, FF = 2, 256, 1024, 2816
TT = SEQ // P
KD = D // P
LC = 64
NC = SEQ // LC
GH, GK, GV, RANK = 4, 64, 128, 16
DH, DE = 8, 64
MH, ME = 4, 128
CONV = 4
EPS = 1e-5
ALPHA = float((2 * LAYERS) ** 0.25)
BIG = 1e30

FG = 256
NG = FF // FG
SLOTS = 3
BW = 2048
FB = 3 * NG
NGRP = 16
B_MIX = FB
B_PROJ = B_MIX + 2 * NGRP
B_OUT = B_PROJ + 6
B_FFN2 = B_OUT + 4
BLOCKS = B_FFN2 + FB
assert B_MIX % SLOTS == 0 and B_FFN2 % SLOTS == 0 and BLOCKS % SLOTS == 0
SM = 68
(G_GQK, G_GV, G_GR, G_DQ, G_DK, G_DV, G_MQ, G_MK, G_MV, G_MO, G_GATE) = range(11)

GATE_GRPS = NGRP - G_GATE

C_ID, C_TRI, C_SUF, C_OFF, C_DIST, C_LNC, C_SEL = 0, 128, 256, 384, 512, 896, 1280
C_W = C_SEL + MH * P
V_GG, V_MG, V_BA, V_W = 0, 512, 1024, 1280


def trunk(nc, x_in, stream, consts, lnp, vecs, bgate, wsmall, wa2, bif, convp, out):
    with ExitStack() as ctx:
        def sb(name, shape, dt=F32):
            return ctx.enter_context(nc.sbuf_tensor(name, shape, dt))

        def sem(name):
            return ctx.enter_context(nc.semaphore(name))

        raw = sb("raw", [P, SLOTS, BW])
        hi = sb("hi", [P, SLOTS, BW], F32R)
        lo = sb("lo", [P, SLOTS, BW], F32R)
        X = sb("X", [P, TT, D])
        U = sb("U", [P, TT, D])
        xTh = sb("xTh", [P, KD, SEQ], F32R)
        xTl = sb("xTl", [P, KD, SEQ], F32R)
        hTh = sb("hTh", [P, KD * SM], F32R)
        hTl = sb("hTl", [P, KD * SM], F32R)
        fscr = sb("fscr", [P, MH * (CONV - 1 + SEQ)])
        fsil = fscr[:, 0:TT * FG].rearrange("p (t n) -> p t n", t=TT)
        fh = fscr[:, TT * FG:2 * TT * FG].rearrange("p (t n) -> p t n", t=TT)
        cin = fscr[:, :].rearrange("p (h n) -> p h n", h=MH)
        pln = sb("pln", [P, 2 * D])
        vec = sb("vec", [P, V_W])
        bg = sb("bg", [P, 2, 512])
        cst = sb("cst", [P, C_W])
        cvp = sb("cvp", [P, 2 * MH, CONV + 1])
        bif_t = sb("bif_t", [MH, 2])
        gates = sb("gates", [P, TT, 3 * D])
        gv = sb("gv", [P, TT, 512])
        gr = sb("gr", [P, TT, 512])
        dv = sb("dv", [P, TT, 512])
        mv1 = sb("mv1", [P, TT, MH, ME + 1])
        mo = sb("mo", [P, TT, 512])
        R2 = sb("R2", [P, 4644])
        bh = sb("bh", [P, 384])
        emr = sb("emr", [MH, SEQ])
        small = sb("small", [P, 220])
        ones = sb("ones", [MH, LC])
        qkT = pln[:, :].rearrange("p (j n) -> p j n", j=2 * MH)
        T0 = U[:, 0, :].rearrange("p (t n) -> p t n", t=TT)
        T1 = U[:, 1, :].rearrange("p (t n) -> p t n", t=TT)
        gscr = gates[:, :, :].rearrange("p t n -> p (t n)")
        la, le = gscr[:, 0:512], gscr[:, 512:1024]
        E1, E2, E3 = (gscr[:, 1024 + 512 * i:1536 + 512 * i] for i in range(3))
        qdT, kiT, kd = (gscr[:, 2560 + 512 * i:3072 + 512 * i] for i in range(3))
        attm = gscr[:, 4096:5120].rearrange("p (q n) -> p q n", q=2)
        gst = gscr[:, 5120:5888].rearrange("p (c a n) -> p c a n", c=NC - 1, a=2)
        aT = gscr[0:RANK, 5888:6144]
        gyn = gscr[:, 1024:2048].rearrange("p (t n) -> p t n", t=TT)
        dqT = R2[:, 0:1024].rearrange("p (a n) -> p a n", a=4)
        dkT = R2[:, 1024:2048].rearrange("p (a n) -> p a n", a=4)
        dL, dPT = R2[:, 2048:2432], R2[:, 2432:2816]
        wsm_raw = R2[:, 0:KD * SM]
        wa2_t = R2[0:RANK, 544:800]
        G_, gf, F_, M_, WI, WK = (R2[0:MH, 3096 + 256 * i:3352 + 256 * i] for i in range(6))
        EM = emr[:, :]
        mA = R2[:, 0:1024].rearrange("p (t n) -> p t n", t=TT)
        mkw = R2[:, 1024:2048].rearrange("p (t n) -> p t n", t=TT)
        qwT = R2[:, 2048:3072].rearrange("p (h n) -> p h n", h=MH)
        mcs = R2[:, 3096:3096 + 3 * MH * (ME + 1)].rearrange("p (c h n) -> p c h n", c=NC - 1, h=MH)
        st = small[:, 0:48].rearrange("p (a n) -> p a n", n=6)
        mv = small[:, 48:64].rearrange("p (a n) -> p a n", n=2)
        vv, rs, rt = small[:, 64:72], small[:, 72:80], small[:, 80:88]
        dmax = small[:, 88:90]
        dsum = small[:, 90:106].rearrange("p (t h) -> p t h", t=TT)
        drec = small[:, 106:122].rearrange("p (t h) -> p t h", t=TT)
        mc = small[:, 122:154].rearrange("p (t q h) -> p t q h", t=TT, q=4)
        ac = small[:, 154:170].rearrange("p (h c) -> p h c", h=MH)
        md = small[:, 72:80]
        ma = small[:, 80:88]
        lst = small[:, 184:184 + 12 * TT].rearrange("p (t a n) -> p t a n", t=TT, a=2)
        lmv = small[:, 208:208 + 2 * TT].rearrange("p (t n) -> p t n", t=TT)
        std, rstd = small[:, 212:212 + TT], small[:, 214:214 + TT]
        eps_t, warm, zero = small[:, 216:218], small[:, 218:219], small[:, 219:220]
        mprev = small[0:MH, 172:172 + NC + 1]
        ones4 = ones[0:MH, :]
        ident = cst[:, C_ID:C_ID + P]
        tri = cst[:, C_TRI:C_TRI + P]
        B = [ctx.enter_context(nc.psum_tensor(f"bank{i}", [P, 512], F32)) for i in range(8)]

        s_x_in = [sem(f"x_loaded{tt}") for tt in range(TT)]
        s_ident = sem("identity_loaded")
        s_eps = sem("epsilons_set")
        s_cst = sem("consts_loaded")
        s_par = sem("layer_params_loaded")
        s_pln = sem("norm_params_loaded")
        s_bg = [sem(f"gate_bias_loaded{i}") for i in range(2)]
        s_raw = [sem(f"raw_loaded{i}") for i in range(SLOTS)]
        s_hi = sem("hi_split")
        s_lo = sem("lo_split")
        s_used = sem("block_used")
        s_x = sem("x_ready")
        s_var = sem("ln_variance")
        s_std = sem("ln_std")
        s_xt = sem("x_transposed")
        s_xh = sem("xT_hi")
        s_xl = sem("xT_lo")
        s_gu = sem("gate_up_done")
        s_sil = sem("silu_done")
        s_h = sem("h_ready")
        s_ht = sem("h_transposed")
        s_hh = sem("hT_hi")
        s_hl = sem("hT_lo")
        s_acc = sem("sublayer_tile0")
        s_out = sem("out_stored")
        s_small_ps = sem("small_ps")
        s_gla_gate_ps = sem("gla_gate_ps")
        s_gla_cum = sem("gla_cum")
        s_gla_scores = sem("gla_scores")
        s_gla_out = sem("gla_out")
        s_dil_q_T = sem("dil_q_T")
        s_dil_k_T = sem("dil_k_T")
        s_ml_q_T = sem("ml_q_T")
        s_ml_k_T = sem("ml_k_T")
        s_ml_cols = sem("ml_cols")
        s_ml_max_b = sem("ml_max_b")
        s_ml_scores = sem("ml_scores")
        s_ml_k_nat = sem("ml_k_nat")
        s_ml_inter_b = sem("ml_inter_b")
        s_ml_kv = sem("ml_kv")
        s_yT = sem("yT")
        s_merged_T = sem("merged_T")
        s_group0 = sem("group0")
        s_dil_pv = sem("dil_pv")
        s_dil_p_T = sem("dil_p_T")
        s_dil_scores = sem("dil_scores")
        s_ml_out = sem("ml_out")
        s_small_hi = sem("small_hi")
        s_group_out = sem("group_out")
        s_softplus = sem("softplus")
        s_gla_decay = sem("gla_decay")
        s_ml_rows_exp = sem("ml_rows_exp")
        s_dil_qT = sem("dil_qT")
        s_dil_kT = sem("dil_kT")
        s_conv_in = sem("conv_in")
        s_ml_weights = sem("ml_weights")
        s_y_hi = sem("y_hi")
        s_merged_hi = sem("merged_hi")
        s_gate_sig = sem("gate_sig")
        s_out_gate = sem("out_gate")
        s_dil_pT = sem("dil_pT")
        s_dil_exp = sem("dil_exp")
        s_small_lo = sem("small_lo")
        s_small_out = sem("small_out")
        s_gate_abs = sem("gate_abs")
        s_log_sig = sem("log_sig")
        s_ml_rows = sem("ml_rows")
        s_gla_qk = sem("gla_qk")
        s_gla_state = sem("gla_state")
        s_gla_norm = sem("gla_norm")
        s_dil_y = sem("dil_y")
        s_ml_mc = sem("ml_mc")
        s_conv = sem("conv")
        s_ml_A = sem("ml_A")
        s_ml_q = sem("ml_q")
        s_ml_state = sem("ml_state")
        s_y_lo = sem("y_lo")
        s_merged_lo = sem("merged_lo")
        s_ml_var = sem("ml_var")
        s_ml_std = sem("ml_std")
        s_ml_y = sem("ml_y")
        s_merged = sem("merged")
        s_gates_out = sem("gates_out")
        s_dil_logits = sem("dil_logits")
        block = ctx.enter_context(nc.Block())

        def block_used(eng, l, b):
            eng.wait_ge(s_used, BLOCKS * l + (b + 1 + SLOTS))

        def group_tile_done(eng, l, i, tt):
            if tt == 0:
                eng.wait_ge(s_group0, NGRP * l + (i + 1))
            else:
                block_used(eng, l, B_MIX + 2 * i + 1)

        def half_cols(i):
            return slice(512 * i, 512 * i + 512)

        @block.sync
        def _(sp):
            sp.dma_start(ident, consts[:, C_ID:C_ID + P]).then_inc(s_ident, 16)
            for s in range(SLOTS):
                sp.dma_start(raw[:, s, :], stream[s]).then_inc(s_raw[s], 16)
                if s < TT:
                    sp.dma_start(X[:, s, :], x_in[P * s:P * s + P, :]).then_inc(s_x_in[s], 16)
            sp.dma_start(cst[:, C_TRI:], consts[:, C_TRI:]).then_inc(s_cst, 16)
            with sp.Fori(1, LAYERS * BLOCKS // SLOTS) as i:
                for s in range(SLOTS):
                    sp.wait_ge(s_lo, SLOTS * i + (s - SLOTS + 1))
                    sp.dma_start(raw[:, s, :], stream[SLOTS * i + s]).then_inc(s_raw[s], 16)
            sp.wait_ge(s_lo, LAYERS * BLOCKS - SLOTS + 1)
            sp.dma_start(raw[:, 0, :], stream[0]).then_inc(s_raw[0], 16)
            for tt in range(TT):
                for hf in range(2):
                    sp.wait_ge(s_x, 2 * TT * 3 * LAYERS + 2 * tt + hf + 1)
                    sp.dma_start(out[P * tt:P * tt + P, half_cols(hf)], X[:, tt, half_cols(hf)]).then_inc(s_out, 16)
            sp.wait_ge(s_out, 2 * 16 * TT)

        @block.gpsimd
        def _(pool):
            nc.gpsimd.memset(eps_t[:, 1:2], EPS)
            nc.gpsimd.memset(eps_t[:, 0:1], 4 * EPS).then_inc(s_eps, 1)
            for tt in range(TT):
                for hf in range(2):
                    pool.wait_ge(s_x_in[tt], 16)
                    nc.gpsimd.memset(drec[:, tt, hf:hf + 1], 0.0).then_inc(s_x, 1)

        @block.scalar
        def _(act):
            def split_hi(n, m, s):
                act.wait_ge(s_raw[s], 16 * m + 16)
                act.wait_ge(s_used, n + 1)
                nc.scalar.copy(hi[:, s, :], raw[:, s, :]).then_inc(s_hi, 1)

            def split_layer_hi(l, b):
                split_hi(BLOCKS * l + b, (BLOCKS // SLOTS) * l + b // SLOTS, b % SLOTS)

            def split_xT_hi(r, tt):
                for hf in range(2):
                    act.wait_ge(s_xt, 2 * TT * r + (2 * tt + hf + 1))
                    nc.scalar.copy(xTh[:, 4 * hf:4 * hf + 4, P * tt:P * tt + P],
                                   B[2 + hf][:, :].rearrange("p (c n) -> p c n", c=4)).then_inc(s_xh, 1)

            def layer_norm_std(r, q, tt):
                act.wait_ge(s_var, TT * r + (tt + 1))
                nc.scalar.activation(std[:, tt:tt + 1], lmv[:, tt, 1:2], ACT.Sqrt,
                                     bias=eps_t[:, q % 2:q % 2 + 1]).then_inc(s_std, 1)

            def junction(l, q, b):
                layer_norm_std(3 * l + q, q, 0)
                split_layer_hi(l, b + 1)
                split_xT_hi(3 * l + q + 1, 0)
                layer_norm_std(3 * l + q, q, 1)
                split_xT_hi(3 * l + q + 1, 1)
                split_layer_hi(l, b + 2)

            def ffn_group(l, f, g, base, splits=SLOTS, peeled=False, final=False):
                it = (2 * NG) * l + (NG * f) + g
                n0 = BLOCKS * l + base + SLOTS * g + SLOTS
                for tt in range(TT):
                    if tt == 0:
                        act.wait_ge(s_gu, it + 1)
                    else:
                        act.wait_ge(s_used, n0 + (2 if peeled else 1))
                    nc.scalar.activation(fsil[:, tt, :], B[tt][:, 0:FG], ACT.Silu).then_inc(s_sil, 1)
                m = (BLOCKS // SLOTS) * l + (base // SLOTS + 1) + g
                if splits:
                    split_hi(n0, m, 0)
                act.wait_ge(s_ht, it + 1)
                if final:
                    nc.scalar.copy(xTh[:, 0:2, :], B[2][:, :].rearrange("p (c n) -> p c n", c=2)).then_inc(s_hh, 1)
                    nc.scalar.activation(warm, eps_t[:, 0:1], ACT.Sqrt)
                else:
                    nc.scalar.copy(hTh[:, 0:512], B[2][:, :]).then_inc(s_hh, 1)
                for i in range(1, splits):
                    split_hi(n0 + i, m, i)

            def evac_group(l, i):
                dst = {G_GQK: T0, G_GV: gv, G_GR: gr, G_DQ: T1, G_DK: T0, G_DV: dv, G_MQ: T1,
                       G_MK: T0, G_MO: mo}.get(i)
                if i == G_DK:
                    act.wait_ge(s_gla_qk, l + 1)
                if i == G_MQ:
                    act.wait_ge(s_dil_q_T, l + 1)
                if i == G_MK:
                    act.wait_ge(s_dil_k_T, l + 1)
                for tt in range(TT):
                    group_tile_done(act, l, i, tt)
                    ps = B[2 * (i % 2) + tt]
                    if i == G_MV:
                        last = nc.scalar.copy(mv1[:, tt, :, 0:ME], ps[:, :].rearrange("p (h n) -> p h n", h=MH))
                    elif i == G_GR:
                        last = nc.scalar.activation(gr[:, tt, :], ps[:, :], ACT.Silu)
                    else:
                        last = nc.scalar.copy(dst[:, tt, :], ps[:, :])
                last.then_inc(s_group_out, 1)

            def load_gate_bias(l, i):
                act.dma_start(bg[:, i % 2, :],
                              bgate[l, 512 * i:512 * i + 512].partition_broadcast(P)).then_inc(s_bg[i % 2], 16)

            def load_norm(l, q):
                act.dma_start(pln[:, :], lnp[l, q, :].partition_broadcast(P)).then_inc(s_pln, 16)

            act.wait_ge(s_eps, 1)
            nc.scalar.activation(warm, eps_t[:, 0:1], ACT.Sqrt)
            split_hi(0, 0, 0)
            split_xT_hi(0, 0)
            with act.Fori(0, LAYERS) as l:
                split_layer_hi(l, 1)
                split_xT_hi(3 * l, 1)
                split_layer_hi(l, 2)
                nc.scalar.activation(warm, eps_t[:, 0:1], ACT.Silu)
                act.dma_start(vec[:, :], vecs[l].partition_broadcast(P)).then_inc(s_par, 16)
                act.dma_start(wsm_raw, wsmall[l]).then_inc(s_par, 16)
                act.dma_start(wa2_t, wa2[l]).then_inc(s_par, 16)
                act.dma_start(bif_t[:, :], bif[l]).then_inc(s_par, 16)
                act.dma_start(cvp[:, :, :], convp[l]).then_inc(s_par, 16)
                load_norm(l, 0)
                ffn_group(l, 0, 0, 0, peeled=True)
                with act.Fori(1, NG - 1) as g:
                    ffn_group(l, 0, g, 0)
                ffn_group(l, 0, NG - 1, 0, splits=1, final=True)
                junction(l, 0, B_MIX)
                act.wait_ge(s_par, (5 * 16) * l + 80)
                nc.scalar.copy(hTh[:, :], wsm_raw).then_inc(s_small_hi, 1)
                load_gate_bias(l, 0)
                load_gate_bias(l, 1)
                def split_y_hi(turned, copied, n, i, b0, c0):
                    act.wait_ge(turned, n * l + (i + 1))
                    for tt in range(TT):
                        last = nc.scalar.copy(xTh[:, c0:c0 + 4, P * tt:P * tt + P],
                                              B[b0 + tt][:, :].rearrange("p (c n) -> p c n", c=4))
                    last.then_inc(copied, 1)

                def sigmoid_gates(b):
                    act.wait_ge(s_gates_out, GATE_GRPS * l + (2 * b + 2))
                    nc.scalar.activation(gates[:, :, D * b:D * b + D], gates[:, :, D * b:D * b + D],
                                                    ACT.Sigmoid).then_inc(s_gate_sig, 1)

                for k in range(2 * NGRP):
                    if k % 2 and k // 2 < G_GATE:
                        evac_group(l, k // 2)
                    if k == 2:
                        act.wait_ge(s_gate_abs, l + 1)
                        nc.scalar.activation(le, le, ACT.Exp, scale=-1.0)
                        nc.scalar.activation(EM, EM, ACT.Exp, scale=-1.0)
                        act.drain()
                        nc.scalar.activation(le, le, ACT.Ln, bias=1.0)
                        nc.scalar.activation(EM, EM, ACT.Ln, bias=1.0).then_inc(s_softplus, 1)
                    if k == 4:
                        act.wait_ge(s_gla_cum, l + 1)
                        s = 1.0 / 16.0
                        nc.scalar.activation(E1, B[4][:, :], ACT.Exp, scale=s)
                        nc.scalar.activation(E2, B[4][:, :], ACT.Exp, scale=-s)
                        nc.scalar.activation(E3, B[5][:, :], ACT.Exp, scale=s).then_inc(s_gla_decay, 1)
                    if k == 5:
                        act.wait_ge(s_ml_rows, l + 1)
                        nc.scalar.activation(WI, WI, ACT.Exp, scale=-1.0)
                        nc.scalar.activation(WK, WK, ACT.Exp)
                        nc.scalar.activation(EM, EM, ACT.Exp, scale=-1.0).then_inc(s_ml_rows_exp, 1)
                    if k in (10, 11):
                        turned, dst, b0, copied = ((s_dil_q_T, dqT, 6, s_dil_qT) if k == 10 else
                                                    (s_dil_k_T, dkT, 4, s_dil_kT))
                        act.wait_ge(turned, l + 1)
                        for tt in range(TT):
                            last = nc.scalar.copy(dst[:, :, P * tt:P * tt + P],
                                                  B[b0 + tt][:, :].rearrange("p (c n) -> p c n", c=4))
                        last.then_inc(copied, 1)
                    h = k - 12
                    if 0 <= h - 1 < DH:
                        act.wait_ge(s_dil_p_T, DH * l + h)
                        nc.scalar.copy(dPT, B[5][:, 0:384]).then_inc(s_dil_pT, 1)
                    if 0 <= h < DH:
                        act.wait_ge(s_dil_logits, DH * l + (h + 1))
                        nc.scalar.activation(dL[:, 0:P], dL[:, 0:P], ACT.Exp, bias=dmax[:, 0:1],
                                             accum_out=dsum[:, 0, h:h + 1])
                        nc.scalar.activation(dL[:, P:3 * P], dL[:, P:3 * P], ACT.Exp,
                                             bias=dmax[:, 1:2], accum_out=dsum[:, 1, h:h + 1]).then_inc(s_dil_exp, 1)
                    if k in (22, 24):
                        act.wait_ge(s_ml_q_T if k == 22 else s_ml_k_T, l + 1)
                        if k == 24:
                            act.wait_ge(s_conv, 2 * l + 1)
                            nc.scalar.activation(qkT[:, 0:MH, :], qkT[:, 0:MH, :], ACT.Silu)
                        for tt in range(TT):
                            last = nc.scalar.copy(cin[:, :, CONV - 1 + P * tt:CONV - 1 + P * tt + P],
                                                  B[4 + tt][:, :].rearrange("p (h n) -> p h n", h=MH))
                        last.then_inc(s_conv_in, 1)
                    if k == 25:
                        act.wait_ge(s_conv, 2 * l + 2)
                        nc.scalar.activation(qkT[:, MH:, :], qkT[:, MH:, :], ACT.Silu)
                        act.wait_ge(s_ml_max_b, l + 1)
                        act.wait_ge(s_ml_mc, l + 1)
                        for tt in range(TT):
                            for hh in range(MH):
                                last = nc.scalar.activation(mA[:, tt, P * hh:P * hh + P],
                                                            B[4 + tt][:, P * hh:P * hh + P], ACT.Exp,
                                                            bias=mc[:, tt, 0, hh:hh + 1], scale=-1.0)
                        last.then_inc(s_ml_weights, 1)
                    if k % 2 and G_GATE <= k // 2 < NGRP - 2:
                        i = k // 2
                        act.wait_ge(s_gates_out, GATE_GRPS * l + (i - G_GATE + 1))
                        load_gate_bias(l, i - G_GATE + 2)
                    if k == 29:
                        act.wait_ge(s_ml_q, l + 1)
                        load_norm(l, 1)
                    if k == 2 * NGRP - 1:
                        split_y_hi(s_yT, s_y_hi, 3, 0, 0, 0)
                    split_layer_hi(l, B_MIX + k + SLOTS)
                    if k == 20:
                        nc.scalar.activation(mo[:, :, :], mo[:, :, :], ACT.Sigmoid).then_inc(s_out_gate, 1)
                    if k == 30:
                        sigmoid_gates(0)
                        sigmoid_gates(1)

                sigmoid_gates(2)
                split_y_hi(s_yT, s_y_hi, 3, 1, 2, 4)
                nc.scalar.activation(warm, eps_t[:, 0:1], ACT.Sqrt)
                act.wait_ge(s_ml_var, l + 1)
                nc.scalar.activation(ma, ma, ACT.Sqrt).then_inc(s_ml_std, 1)
                for i in range(2):
                    split_layer_hi(l, B_PROJ + SLOTS + i)
                split_y_hi(s_yT, s_y_hi, 3, 2, 4, 0)
                for i in range(2, 5):
                    split_layer_hi(l, B_PROJ + SLOTS + i)
                split_y_hi(s_merged_T, s_merged_hi, 2, 0, 0, 4)
                split_layer_hi(l, B_PROJ + SLOTS + 5)
                split_y_hi(s_merged_T, s_merged_hi, 2, 1, 2, 0)
                for i in range(2):
                    split_layer_hi(l, B_OUT + SLOTS + i)
                junction(l, 1, B_FFN2)
                nc.scalar.activation(warm, eps_t[:, 0:1], ACT.Silu)
                load_norm(l, 2)
                ffn_group(l, 1, 0, B_FFN2, peeled=True)
                with act.Fori(1, NG - 1) as g:
                    ffn_group(l, 1, g, B_FFN2)
                ffn_group(l, 1, NG - 1, B_FFN2, splits=1, final=True)
                layer_norm_std(3 * l + 2, 2, 0)
                split_xT_hi(3 * l + 3, 0)
                layer_norm_std(3 * l + 2, 2, 1)

        @block.vector
        def _(dve):
            v = nc.vector

            def split_lo(n, s):
                dve.wait_ge(s_hi, n + 1)
                v.tensor_tensor(lo[:, s, :], raw[:, s, :], hi[:, s, :].bitcast(F32),
                                ALU.subtract).then_inc(s_lo, 1)

            def split_layer_lo(l, b):
                split_lo(BLOCKS * l + b, b % SLOTS)

            def lo_of_bank(c0, tt, bank):
                return v.tensor_tensor(xTl[:, c0:c0 + 4, P * tt:P * tt + P],
                                       bank[:, :].rearrange("p (c n) -> p c n", c=4),
                                       xTh[:, c0:c0 + 4, P * tt:P * tt + P].bitcast(F32), ALU.subtract)

            def split_xT_lo(r, tt, hf):
                dve.wait_ge(s_xh, 2 * TT * r + (2 * tt + hf + 1))
                lo_of_bank(4 * hf, tt, B[2 + hf]).then_inc(s_xl, 1)

            def ffn_group(l, f, g, base, splits=SLOTS, final=False):
                it = (2 * NG) * l + (NG * f) + g
                for tt in range(TT):
                    dve.wait_ge(s_sil, TT * it + (tt + 1))
                    v.tensor_tensor(fh[:, tt, :], fsil[:, tt, :], B[tt][:, FG:2 * FG], ALU.mult).then_inc(s_h, 1)
                n0 = BLOCKS * l + base + SLOTS * g + SLOTS
                if splits and not final:
                    split_lo(n0, 0)
                dve.wait_ge(s_hh, it + 1)
                if final:
                    v.tensor_tensor(xTl[:, 0:2, :], B[2][:, :].rearrange("p (c n) -> p c n", c=2),
                                    xTh[:, 0:2, :].bitcast(F32), ALU.subtract).then_inc(s_hl, 1)
                else:
                    v.tensor_tensor(hTl[:, 0:512], B[2][:, :], hTh[:, 0:512].bitcast(F32),
                                    ALU.subtract).then_inc(s_hl, 1)
                for i in range(0 if final else 1, splits):
                    split_lo(n0 + i, i)

            def rsqrt(n, var, eps):
                a, y, t = vv[:, 0:n], rs[:, 0:n], rt[:, 0:n]
                v.tensor_scalar(a, var, eps, None, ALU.add)
                dve.drain()
                v.tensor_scalar(y.bitcast(I32), a.bitcast(I32), 1, None, ALU.logical_shift_right)
                dve.drain()
                v.tensor_scalar(y.bitcast(I32), y.bitcast(I32), -1.0, float(0x5F3759DF), ALU.mult, ALU.add)
                for _ in range(3):
                    dve.drain()
                    v.tensor_tensor(t, y, y, ALU.mult)
                    dve.drain()
                    v.scalar_tensor_tensor(t, t, -0.5, a, ALU.mult, ALU.mult)
                    dve.drain()
                    v.scalar_tensor_tensor(y, t, 1.5, y, ALU.add, ALU.mult)
                dve.drain()

            def ln_sum(l, q, tt, hf):
                if tt == 0:
                    dve.wait_ge(s_acc, 6 * l + (2 * q + hf + 1))
                elif hf == 0:
                    block_used(dve, l, (B_MIX, B_FFN2, BLOCKS)[q] - 1)
                v.scalar_tensor_tensor(U[:, tt, half_cols(hf)], X[:, tt, half_cols(hf)],
                                       ALPHA if q == 1 else 2 * ALPHA,
                                       B[4 + 2 * tt + hf][:, :], ALU.mult, ALU.add)

            def ln_stats(tt, hf):
                dve.drain()
                v.bn_stats(lst[:, tt, hf, :], U[:, tt, half_cols(hf)])

            def ln_output(l, q, tt):
                dve.drain()
                v.bn_aggr(lmv[:, tt, :], lst[:, tt, :, :]).then_inc(s_var, 1)
                dve.drain()
                dve.wait_ge(s_pln, 48 * l + (16 * q + 16))
                for hf in range(2):
                    v.scalar_tensor_tensor(U[:, tt, half_cols(hf)], U[:, tt, half_cols(hf)], lmv[:, tt, 0:1],
                                           pln[:, half_cols(hf)], ALU.subtract, ALU.mult)
                    if hf == 0:
                        dve.wait_ge(s_std, (3 * TT) * l + (TT * q + tt + 1))
                        v.reciprocal(rstd[:, tt:tt + 1], std[:, tt:tt + 1])
                    dve.drain()
                    v.scalar_tensor_tensor(X[:, tt, half_cols(hf)], U[:, tt, half_cols(hf)], rstd[:, tt:tt + 1],
                                           pln[:, D + 512 * hf:D + 512 * hf + 512],
                                           ALU.mult, ALU.add).then_inc(s_x, 1)

            def junction(l, q, b):
                for hf in range(2):
                    ln_sum(l, q, 0, hf)
                    ln_stats(0, hf)
                ln_output(l, q, 0)
                for hf in range(2):
                    ln_sum(l, q, 1, hf)
                    split_xT_lo(3 * l + q + 1, 0, hf)
                split_layer_lo(l, b + 1)
                for hf in range(2):
                    ln_stats(1, hf)
                ln_output(l, q, 1)
                for hf in range(2):
                    split_xT_lo(3 * l + q + 1, 1, hf)
                split_layer_lo(l, b + 2)

            def head_norm(srcs, dsts):
                n = len(srcs)
                for i, s in enumerate(srcs):
                    v.bn_stats(st[:, i, :], s)
                dve.drain()
                for i in range(n):
                    v.bn_aggr(mv[:, i, :], st[:, i:i + 1, :])
                dve.drain()
                rsqrt(n, mv[:, 0:n, 1], EPS)
                for i in range(n):
                    last = v.tensor_scalar(dsts[i], srcs[i], mv[:, i, 0:1], rs[:, i:i + 1],
                                           ALU.subtract, ALU.mult)
                return last

            v.memset(mprev[:, 0:1], 0.0)
            v.memset(ones4, 1.0)
            v.memset(mv1[:, :, :, ME:ME + 1], 1.0)

            split_lo(0, 0)
            for hf in range(2):
                split_xT_lo(0, 0, hf)
            with dve.Fori(0, LAYERS) as l:
                split_layer_lo(l, 1)
                for hf in range(2):
                    split_xT_lo(3 * l, 1, hf)
                split_layer_lo(l, 2)
                ffn_group(l, 0, 0, 0)
                with dve.Fori(1, NG - 1) as g:
                    ffn_group(l, 0, g, 0)
                ffn_group(l, 0, NG - 1, 0, splits=1, final=True)
                junction(l, 0, B_MIX)

                def split_y_lo(copied, split, n, i, b0, c0):
                    dve.wait_ge(copied, n * l + (i + 1))
                    for tt in range(TT):
                        last = lo_of_bank(c0, tt, B[b0 + tt])
                    last.then_inc(split, 1)

                dve.wait_ge(s_cst, 16)
                dve.wait_ge(s_small_hi, l + 1)
                v.tensor_tensor(hTl[:, :], wsm_raw, hTh[:, :].bitcast(F32), ALU.subtract).then_inc(s_small_lo, 1)
                for k in range(2 * NGRP):
                    if k % 2 and k // 2 >= G_GATE:
                        i = k // 2
                        j = i - G_GATE
                        dve.wait_ge(s_bg[j % 2], 48 * l + (16 * (j // 2) + 16))
                        for tt in range(TT):
                            group_tile_done(dve, l, i, tt)
                            last = v.tensor_tensor(gates[:, tt, 512 * j:512 * j + 512], B[2 * (i % 2) + tt][:, :],
                                                   bg[:, j % 2, :], ALU.add)
                        last.then_inc(s_gates_out, 1)
                    if k == 1:
                        dve.wait_ge(s_small_ps, l + 1)
                        v.tensor_copy(aT, B[4][0:RANK, 0:SEQ]).then_inc(s_small_out, 1)
                        v.tensor_copy(G_, B[4][32:32 + MH, 0:SEQ])
                        v.tensor_copy(gf, B[4][64:64 + MH, 0:SEQ])
                        v.memset(attm, 0.0)
                        v.memset(cin[:, :, 0:CONV - 1], 0.0)
                        dve.drain()
                        v.tensor_scalar(G_, G_, bif_t[:, 0:1], None, ALU.add)
                        v.tensor_scalar(gf, gf, bif_t[:, 1:2], None, ALU.add)
                    if k == 2:
                        dve.wait_ge(s_gla_gate_ps, l + 1)
                        v.tensor_tensor(la.rearrange("p (t n) -> p t n", t=TT),
                                        B[5][:, :].rearrange("p (t n) -> p t n", t=TT),
                                        vec[:, V_BA:V_BA + 256].unsqueeze(1).to_broadcast([P, TT, 256]), ALU.add)
                        dve.drain()
                        v.scalar_tensor_tensor(le, la, -1.0, la, ALU.mult, ALU.max)
                        v.scalar_tensor_tensor(EM, gf, -1.0, gf, ALU.mult, ALU.max).then_inc(s_gate_abs, 1)
                        dve.wait_ge(s_softplus, l + 1)
                        v.scalar_tensor_tensor(la, la, 0.0, le, ALU.min, ALU.subtract).then_inc(s_log_sig, 1)
                    if k == 3:
                        v.scalar_tensor_tensor(gf, gf, 0.0, EM, ALU.min, ALU.subtract)
                        dve.drain()
                        for c in range(NC):
                            cs = slice(LC * c, LC * c + LC)
                            v.tensor_tensor_scan(F_[:, cs], ones4, gf[:, cs], 0.0, ALU.mult, ALU.add)
                        dve.drain()
                        v.tensor_tensor(G_, G_, F_, ALU.subtract)
                        dve.drain()
                        for c in range(NC):
                            cs = slice(LC * c, LC * c + LC)
                            end = LC * c + LC - 1
                            v.tensor_tensor_scan(M_[:, cs], G_[:, cs], G_[:, cs], mprev[:, c:c + 1],
                                                 ALU.max, ALU.max)
                            dve.drain()
                            v.tensor_tensor(mprev[:, c + 1:c + 2], F_[:, end:end + 1], M_[:, end:end + 1], ALU.add)
                            v.tensor_scalar(WI[:, cs], M_[:, cs], mprev[:, c:c + 1], None, ALU.subtract)
                            v.tensor_scalar(WK[:, cs], G_[:, cs], M_[:, end:end + 1], None, ALU.subtract)
                            dve.drain()
                        v.tensor_tensor(EM, F_, M_, ALU.add).then_inc(s_ml_rows, 1)
                    if k == 4:
                        dve.wait_ge(s_gla_decay, l + 1)
                        v.scalar_tensor_tensor(qdT, B[6][:, :], GK ** -0.5, E1, ALU.mult, ALU.mult)
                        v.tensor_tensor(kiT, B[7][:, :], E2, ALU.mult)
                        v.tensor_tensor(kd.rearrange("p (t n) -> p t n", t=TT), T0[:, :, 256:512],
                                                   E3.rearrange("p (t n) -> p t n", t=TT), ALU.mult).then_inc(s_gla_qk, 1)
                    if k == 7:
                        dve.wait_ge(s_gla_scores, l + 1)
                        v.tensor_copy(gst[:, 0, :, :], B[6][:, 0:256].rearrange("p (a n) -> p a n", a=2))
                        for q in range(2):
                            last = v.copy_predicated(attm[:, q, :].rearrange("p (h n) -> p h n", h=GH),
                                                     tri.bitcast(I32).unsqueeze(1).to_broadcast([P, GH, P]),
                                                     B[4 + q][:, :].rearrange("p (h n) -> p h n", h=GH))
                        for c in (1, 2):
                            dve.drain()
                            for a in range(2):
                                kv = B[6 + c % 2][:, 256 * (c // 2) + P * a:256 * (c // 2) + P * a + P]
                                end = SEQ * a + LC * c + LC - 1
                                last = v.scalar_tensor_tensor(gst[:, c, a, :], gst[:, c - 1, a, :],
                                                              E1[:, end:end + 1], kv, ALU.mult, ALU.add)
                        last.then_inc(s_gla_state, 1)
                    if k == 9:
                        split_layer_lo(l, B_MIX + k + SLOTS)
                        dve.wait_ge(s_gla_out, l + 1)
                        tiles = [(tt, h) for tt in range(TT) for h in range(GH)]
                        head_norm([B[4 + h % 2][:, 256 * tt + P * (h // 2):256 * tt + P * (h // 2) + P]
                                              for tt, h in tiles],
                                             [gyn[:, tt, P * h:P * h + P] for tt, h in tiles]).then_inc(s_gla_norm, 1)
                        dve.drain()
                        v.tensor_tensor(gyn, gyn, vec[:, V_GG:V_GG + 512].unsqueeze(1).to_broadcast([P, TT, 512]),
                                        ALU.mult)
                        dve.drain()
                        dve.wait_ge(s_group_out, G_GATE * l + (G_GR + 1))
                        v.tensor_tensor(gr[:, :, :], gyn, gr[:, :, :], ALU.mult)
                    h = k - 12
                    if 0 <= h < DH:
                        v.scalar_tensor_tensor(bh[:, :], cst[:, C_DIST:C_DIST + 384], -(2.0 ** -(h + 1)),
                                               cst[:, C_LNC:C_LNC + 384], ALU.mult, ALU.add)
                        dve.drain()
                        dve.wait_ge(s_dil_scores, DH * l + (h + 1))
                        v.scalar_tensor_tensor(dL, B[4][:, 0:384], DE ** -0.5, bh[:, :], ALU.mult, ALU.add)
                        dve.drain()
                        v.tensor_reduce(dmax[:, 0:1], dL[:, 0:P], AX, ALU.max, negate=True)
                        v.tensor_reduce(dmax[:, 1:2], dL[:, P:3 * P], AX, ALU.max, negate=True).then_inc(s_dil_logits, 1)
                    if k == 22:
                        dve.wait_ge(s_dil_exp, DH * l + DH)
                        v.reciprocal(drec, dsum)
                        dve.drain()
                        dve.wait_ge(s_dil_pv, DH * l + DH)
                        dve.wait_ge(s_ml_q_T, l + 1)
                        for tt in range(TT):
                            last = v.tensor_tensor(T1[:, tt, :].rearrange("p (h n) -> p h n", h=DH),
                                                   B[6 + tt][:, :].rearrange("p (h n) -> p h n", h=DH),
                                                   drec[:, tt, :].unsqueeze(2).to_broadcast([P, DH, DE]), ALU.mult)
                        last.then_inc(s_dil_y, 1)
                    if k == 23:
                        dve.wait_ge(s_ml_cols, l + 1)
                        v.tensor_copy(mc.rearrange("p t q h -> p (t q h)"), B[6][:, 0:32])
                        v.tensor_copy(ac.rearrange("p h c -> p (h c)"), B[7][:, 0:16]).then_inc(s_ml_mc, 1)
                    if k in (23, 24):
                        j0 = 0 if k == 23 else MH
                        dve.wait_ge(s_conv_in, 2 * l + (1 if k == 23 else 2))
                        for i in range(CONV):
                            for j in range(MH):
                                src, dst, w = cin[:, j, i:i + SEQ], qkT[:, j0 + j, :], cvp[:, j0 + j, :]
                                if i == 0:
                                    last = v.tensor_scalar(dst, src, w[:, 0:1], w[:, CONV:CONV + 1],
                                                           ALU.mult, ALU.add)
                                else:
                                    last = v.scalar_tensor_tensor(dst, src, w[:, i:i + 1], dst, ALU.mult, ALU.add)
                            if i < CONV - 1:
                                dve.drain()
                        last.then_inc(s_conv, 1)
                    if k == 27:
                        dve.wait_ge(s_ml_weights, l + 1)
                        v.memset(zero, 0.0)
                        dve.drain()
                        for tt in range(TT):
                            v.copy_predicated(mA[:, tt, :].rearrange("p (h n) -> p h n", h=MH),
                                              cst[:, C_OFF:C_OFF + P].bitcast(I32).unsqueeze(1).to_broadcast([P, MH, P]),
                                              zero.unsqueeze(2).to_broadcast([P, MH, P]))
                        dve.drain()
                        dve.wait_ge(s_ml_scores, l + 1)
                        for tt in range(TT):
                            last = v.scalar_tensor_tensor(mA[:, tt, :], B[4 + tt][:, :], ME ** -0.5, mA[:, tt, :],
                                                          ALU.mult, ALU.mult)
                        last.then_inc(s_ml_A, 1)
                        dve.wait_ge(s_ml_k_nat, l + 1)
                        for tt in range(TT):
                            for hh in range(MH):
                                last = v.tensor_scalar(mkw[:, tt, P * hh:P * hh + P], B[6 + tt][:, P * hh:P * hh + P],
                                                       mc[:, tt, 2, hh:hh + 1], ME ** -0.5, ALU.mult, ALU.mult)
                    if k == 28:
                        dve.wait_ge(s_ml_inter_b, l + 1)
                        for i in range(2):
                            last = v.tensor_tensor(qwT[:, 2 * i:2 * i + 2, :], qkT[:, 2 * i:2 * i + 2, :],
                                                   B[4 + i][:, :].rearrange("p (h n) -> p h n", h=2), ALU.mult)
                        last.then_inc(s_ml_q, 1)
                    if k in (29, 30):
                        h0 = 0 if k == 29 else 2
                        dve.wait_ge(s_ml_kv, 2 * l + (1 if k == 29 else 2))
                        for c in range(NC - 1):
                            for hh in range(2):
                                kv = B[(6, 7, 4)[c]][:, (ME + 1) * hh:(ME + 1) * (hh + 1)]
                                if c == 0:
                                    last = v.tensor_copy(mcs[:, 0, h0 + hh, :], kv)
                                else:
                                    last = v.scalar_tensor_tensor(mcs[:, c, h0 + hh, :], mcs[:, c - 1, h0 + hh, :],
                                                                  ac[:, h0 + hh, c:c + 1], kv, ALU.mult, ALU.add)
                            if c < NC - 2:
                                dve.drain()
                        last.then_inc(s_ml_state, 1)
                    if k == 21:
                        dve.wait_ge(s_out_gate, l + 1)
                        v.tensor_tensor(mo[:, :, :], mo[:, :, :],
                                        vec[:, V_MG:V_MG + 512].unsqueeze(1).to_broadcast([P, TT, 512]), ALU.mult)
                    if k == 2 * NGRP - 1:
                        split_y_lo(s_y_hi, s_y_lo, 3, 0, 0, 0)
                    if k != 9:
                        split_layer_lo(l, B_MIX + k + SLOTS)

                def gate_branch(b, j):
                    block_used(dve, l, B_PROJ + 2 * b + j)
                    dve.wait_ge(s_gate_sig, 3 * l + (b + 1))
                    cols = slice(D * b + 512 * j, D * b + 512 * j + 512)
                    mcol = slice(512 * j, 512 * j + 512)
                    for tt in range(TT):
                        last = v.tensor_tensor(gates[:, tt, cols], gates[:, tt, cols], B[2 * j + tt][:, :], ALU.mult)
                    if b:
                        dve.drain()
                        last = v.tensor_tensor(gates[:, :, mcol], gates[:, :, mcol], gates[:, :, cols], ALU.add)
                    last.then_inc(s_merged, 1)

                heads = [(tt, h, B[4 + 2 * tt + h // 2][:, (ME + 1) * (h % 2):(ME + 1) * (h % 2) + ME])
                         for tt in range(TT) for h in range(MH)]
                dens = [(md[:, MH * tt + 2 * a:MH * tt + 2 * a + 2].unsqueeze(2),
                         B[4 + 2 * tt + a][:, 0:2 * (ME + 1)].rearrange("p (h n) -> p h n", h=2)[:, :, ME:ME + 1],
                         mc[:, tt, 3, 2 * a:2 * a + 2].unsqueeze(2)) for tt in range(TT) for a in range(2)]
                dve.wait_ge(s_ml_out, TT * l + TT)
                for d, den, floor in dens:
                    v.scalar_tensor_tensor(d, den, -1.0, floor, ALU.mult, ALU.max)
                for i, (_, _, num) in enumerate(heads):
                    v.bn_stats(st[:, i, :], num)
                split_y_lo(s_y_hi, s_y_lo, 3, 1, 2, 4)
                dve.drain()
                for d, den, _ in dens:
                    v.tensor_tensor(d, den, d, ALU.max)
                for i in range(len(heads)):
                    v.bn_aggr(mv[:, i, :], st[:, i:i + 1, :])
                dve.drain()
                v.tensor_scalar(md, md, 1e18, None, ALU.min)
                dve.drain()
                v.scalar_tensor_tensor(ma, md, EPS, md, ALU.mult, ALU.mult)
                dve.drain()
                v.tensor_tensor(ma, ma, mv[:, :, 1], ALU.add).then_inc(s_ml_var, 1)
                gate_branch(0, 0)
                dve.drain()
                dve.wait_ge(s_ml_std, l + 1)
                v.reciprocal(md, ma)
                dve.drain()
                for i, (tt, h, num) in enumerate(heads):
                    v.tensor_scalar(mkw[:, tt, P * h:P * h + P], num, mv[:, i, 0:1], md[:, i:i + 1],
                                    ALU.subtract, ALU.mult)
                dve.drain()
                v.tensor_tensor(mo[:, :, :], mkw, mo[:, :, :], ALU.mult).then_inc(s_ml_y, 1)
                split_layer_lo(l, B_PROJ + SLOTS)
                gate_branch(0, 1)
                split_layer_lo(l, B_PROJ + SLOTS + 1)
                gate_branch(1, 0)
                split_y_lo(s_y_hi, s_y_lo, 3, 2, 4, 0)
                split_layer_lo(l, B_PROJ + SLOTS + 2)
                gate_branch(1, 1)
                split_layer_lo(l, B_PROJ + SLOTS + 3)
                gate_branch(2, 0)
                split_y_lo(s_merged_hi, s_merged_lo, 2, 0, 0, 4)
                split_layer_lo(l, B_PROJ + SLOTS + 4)
                gate_branch(2, 1)
                split_layer_lo(l, B_PROJ + SLOTS + 5)
                split_y_lo(s_merged_hi, s_merged_lo, 2, 1, 2, 0)
                for i in range(2):
                    split_layer_lo(l, B_OUT + SLOTS + i)
                junction(l, 1, B_FFN2)
                ffn_group(l, 1, 0, B_FFN2)
                with dve.Fori(1, NG - 1) as g:
                    ffn_group(l, 1, g, B_FFN2)
                ffn_group(l, 1, NG - 1, B_FFN2, splits=1, final=True)
                for hf in range(2):
                    ln_sum(l, 2, 0, hf)
                    ln_stats(0, hf)
                ln_output(l, 2, 0)
                for hf in range(2):
                    ln_sum(l, 2, 1, hf)
                    ln_stats(1, hf)
                    split_xT_lo(3 * l + 3, 0, hf)
                ln_output(l, 2, 1)

        @block.tensor
        def _(pe):
            def mm(*a, start=True, stop=True):
                return nc.tensor.matmul(*a, start=start, stop=stop, skip_group_check=True)

            def mm3(ps, ah, al, wh, wl, start, stop):
                mm(ps, ah, wh, start=start, stop=False)
                mm(ps, ah, wl, start=False, stop=False)
                return mm(ps, al, wh, start=False, stop=stop)

            def wide_tile(s, ps, tt, c0, first, last):
                for c in range(4):
                    w = slice(512 * c, 512 * c + 512)
                    tok = slice(P * tt, P * tt + P)
                    ins = mm3(ps, xTh[:, c0 + c, tok], xTl[:, c0 + c, tok], hi[:, s, w], lo[:, s, w],
                              first and c == 0, last and c == 3)
                return ins

            def wide_block(n, s, psums, c0, first, last, signal=None):
                pe.wait_ge(s_lo, n + 1)
                for tt in range(TT):
                    ins = wide_tile(s, psums[tt], tt, c0, first, last)
                    if signal and tt == 0:
                        signal(ins)
                ins.then_inc(s_used, 1)

            def layer_block(l, b, psums, c0, first, last, signal=None):
                wide_block(BLOCKS * l + b, b % SLOTS, psums, c0, first, last, signal)

            def transpose_x(r, tt):
                for hf in range(2):
                    pe.wait_ge(s_x, 2 * TT * r + (2 * tt + hf + 1))
                    for c in range(4):
                        last = nc.tensor.transpose(B[2 + hf][:, P * c:P * c + P],
                                                   X[:, tt, 512 * hf + P * c:512 * hf + P * c + P], ident)
                    last.then_inc(s_xt, 1)

            def first_group(l, r, b, signal):
                for tt in range(TT):
                    if tt:
                        transpose_x(r, tt)
                    for hf in range(2):
                        pe.wait_ge(s_xl, 2 * TT * r + (2 * tt + hf + 1))
                        if tt == 0:
                            pe.wait_ge(s_lo, BLOCKS * l + (b + hf + 1))
                        ins = wide_tile(hf, B[tt][:, :], tt, 4 * hf, hf == 0, hf == 1)
                        if tt == 0 and hf == 1:
                            signal(ins)
                        if tt == 1:
                            ins.then_inc(s_used, 1)

            def gate_up(n, s0, s1):
                wide_block(n, s0, (B[0][:, :], B[1][:, :]), 0, True, False)
                wide_block(n + 1, s1, (B[0][:, :], B[1][:, :]), 4, False, True,
                           lambda ins: ins.then_inc(s_gu, 1))

            def transpose_h(it):
                pe.wait_ge(s_h, TT * it + TT)
                for c in range(2):
                    for tt in range(TT):
                        last = nc.tensor.transpose(B[2][:, SEQ * c + P * tt:SEQ * c + P * tt + P],
                                                   fh[:, tt, P * c:P * c + P], ident)
                last.then_inc(s_ht, 1)

            def down_half(s, tt, hf, first=False):
                for c in range(2):
                    a = slice(SEQ * c + P * tt, SEQ * c + P * tt + P)
                    w = slice(D * c + 512 * hf, D * c + 512 * hf + 512)
                    ins = mm3(B[4 + 2 * tt + hf][:, :], hTh[:, a], hTl[:, a], hi[:, s, w], lo[:, s, w],
                              first and c == 0, False)
                return ins

            def final_down_half(s, tt, hf):
                for c in range(2):
                    tok = slice(P * tt, P * tt + P)
                    w = slice(D * c + 512 * hf, D * c + 512 * hf + 512)
                    ins = mm3(B[4 + 2 * tt + hf][:, :], xTh[:, c, tok], xTl[:, c, tok], hi[:, s, w], lo[:, s, w],
                              False, c == 1)
                return ins

            def down(it, n, s, first=False):
                pe.wait_ge(s_lo, n + 1)
                pe.wait_ge(s_hl, it + 1)
                for tt in range(TT):
                    for hf in range(2):
                        ins = down_half(s, tt, hf, first)
                ins.then_inc(s_used, 1)

            def ffn(l, f, base, r):
                it0 = (2 * NG) * l + (NG * f)
                n0 = BLOCKS * l + base
                first_group(l, r, base, lambda ins: ins.then_inc(s_gu, 1))
                pe.wait_ge(s_lo, n0 + 3)
                for tt in range(TT):
                    pe.wait_ge(s_h, TT * it0 + (tt + 1))
                    for c in range(2):
                        ins = nc.tensor.transpose(B[2][:, SEQ * c + P * tt:SEQ * c + P * tt + P],
                                                  fh[:, tt, P * c:P * c + P], ident)
                    if tt:
                        ins.then_inc(s_ht, 1)
                    ins = wide_tile(2, B[tt][:, :], tt, 0, True, False)
                ins.then_inc(s_used, 1)
                wide_block(n0 + 3, 0, (B[0][:, :], B[1][:, :]), 4, False, True,
                           lambda ins: ins.then_inc(s_gu, 1))
                down(it0, n0 + 4, 1, first=True)
                transpose_h(it0 + 1)
                with pe.Fori(2, NG - 1) as g:
                    gate_up(n0 + SLOTS * g - 1, 2, 0)
                    down(it0 + g - 1, n0 + SLOTS * g + 1, 1)
                    transpose_h(it0 + g)
                gate_up(n0 + (FB - 4), 2, 0)
                pe.wait_ge(s_lo, n0 + (FB - 1))
                pe.wait_ge(s_hl, it0 + (NG - 1))
                for hf in range(2):
                    down_half(1, 0, hf)
                transpose_h(it0 + (NG - 1))
                down_half(1, 1, 0)
                pe.wait_ge(s_lo, n0 + FB)
                pe.wait_ge(s_hl, it0 + NG)
                for hf in range(2):
                    final_down_half(2, 0, hf).then_inc(s_acc, 1)
                down_half(1, 1, 1).then_inc(s_used, 1)
                for hf in range(2):
                    ins = final_down_half(2, 1, hf)
                ins.then_inc(s_used, 1)
                transpose_x(r + 1, 0)

            def four_transposes(bank, src):
                for c in range(4):
                    last = nc.tensor.transpose(bank[:, P * c:P * c + P], src[:, P * c:P * c + P], ident)
                return last

            for _ in range(SLOTS):
                pe.nop().then_inc(s_used, 1)
            pe.wait_ge(s_ident, 16)
            transpose_x(0, 0)
            with pe.Fori(0, LAYERS) as l:
                ffn(l, 0, 0, 3 * l)
                first_group(l, 3 * l + 1, B_MIX, lambda ins: ins.then_inc(s_group0, 1))
                pe.wait_ge(s_small_lo, l + 1)
                for c in range(KD):
                    a = slice(SM * c, SM * c + SM)
                    last = mm3(B[4][0:SM, 0:SEQ], hTh[:, a], hTl[:, a], xTh[:, c, :], xTl[:, c, :],
                               c == 0, c == KD - 1)
                last.then_inc(s_small_ps, 1)
                for k in range(2, 2 * NGRP):
                    i = k // 2
                    if k % 2 == 0 and i >= 2:
                        if i - 2 < G_GATE:
                            pe.wait_ge(s_group_out, G_GATE * l + (i - 1))
                        else:
                            pe.wait_ge(s_gates_out, GATE_GRPS * l + (i - 1 - G_GATE))
                    layer_block(l, B_MIX + k, (B[2 * (i % 2)][:, :], B[2 * (i % 2) + 1][:, :]), 4 * (k % 2),
                                k % 2 == 0, k % 2 == 1,
                                (lambda ins: ins.then_inc(s_group0, 1)) if k % 2 else None)
                    if k == 2:
                        pe.wait_ge(s_small_out, l + 1)
                        for tt in range(TT):
                            last = mm(B[5][:, 256 * tt:256 * tt + 256], aT[:, P * tt:P * tt + P], wa2_t)
                        last.then_inc(s_gla_gate_ps, 1)
                    if k == 3:
                        pe.wait_ge(s_group_out, G_GATE * l + (G_GQK + 1))
                        for q in range(2):
                            for a in range(2):
                                for tt in range(TT):
                                    last = nc.tensor.transpose(
                                        B[6 + q][:, SEQ * a + P * tt:SEQ * a + P * tt + P],
                                        T0[:, tt, 256 * q + P * a:256 * q + P * a + P], ident)
                    if k == 4:
                        pe.wait_ge(s_cst, 16)
                        pe.wait_ge(s_log_sig, l + 1)
                        for a in range(2):
                            for tt in range(TT):
                                mm(B[4][:, SEQ * a + P * tt:SEQ * a + P * tt + P],
                                   la[:, 256 * tt + P * a:256 * tt + P * a + P], tri)
                        for tt in range(TT):
                            last = mm(B[5][:, 256 * tt:256 * tt + 256], cst[:, C_SUF:C_SUF + P],
                                      la[:, 256 * tt:256 * tt + 256])
                        last.then_inc(s_gla_cum, 1)
                    if k == 7:
                        pe.wait_ge(s_gla_qk, l + 1)
                        pe.wait_ge(s_group_out, G_GATE * l + (G_GV + 1))
                        for tt in range(TT):
                            for h in range(GH):
                                r0, c0 = GK * (h % 2), SEQ * (h // 2) + P * tt
                                col = 256 * tt + P * (h // 2)
                                last = mm(B[4 + h % 2][:, col:col + P], kiT[r0:r0 + GK, c0:c0 + P],
                                          qdT[r0:r0 + GK, c0:c0 + P])
                        for c in range(NC - 1):
                            tt, r0 = c // 2, LC * (c % 2)
                            for h in range(GH):
                                o0, col = GK * (h % 2), 256 * (c // 2) + P * (h // 2)
                                last = mm(B[6 + c % 2][o0:o0 + GK, col:col + P],
                                          kd[r0:r0 + LC, 256 * tt + GK * h:256 * tt + GK * h + GK],
                                          gv[r0:r0 + LC, tt, GV * h:GV * h + GV])
                        last.then_inc(s_gla_scores, 1)
                    if k == 9:
                        pe.wait_ge(s_gla_state, l + 1)
                        for tt in range(TT):
                            for h in range(GH):
                                col = 256 * tt + P * (h // 2)
                                ps = B[4 + h % 2][:, col:col + P]
                                last = mm(ps, attm[:, h % 2, col:col + P], gv[:, tt, P * h:P * h + P], stop=False)
                                for c in (2 * tt, 2 * tt + 1):
                                    if c:
                                        r0, o0 = GK * (h % 2), LC * (c % 2)
                                        q0 = SEQ * (h // 2) + LC * c
                                        last = mm(B[4 + h % 2][o0:o0 + LC, col:col + P],
                                                  qdT[r0:r0 + GK, q0:q0 + LC],
                                                  gst[r0:r0 + GK, c - 1, h // 2, :], start=False)
                        last.then_inc(s_gla_out, 1)
                    if k in (10, 11):
                        src, b0, g = (T1, 6, G_DQ) if k == 10 else (T0, 4, G_DK)
                        pe.wait_ge(s_group_out, G_GATE * l + (g + 1))
                        pe.wait_ge(s_gla_state if k == 10 else s_gla_norm, l + 1)
                        for tt in range(TT):
                            last = four_transposes(B[b0 + tt], src[:, tt, :])
                        last.then_inc(s_dil_q_T if k == 10 else s_dil_k_T, 1)
                    h = k - 12
                    if 0 <= h - 2 < DH:
                        g = h - 2
                        pe.wait_ge(s_dil_pT, DH * l + (g + 1))
                        if g == 0:
                            pe.wait_ge(s_group_out, G_GATE * l + (G_DV + 1))
                        cols = slice(DE * g, DE * g + DE)
                        mm(B[6][:, cols], dPT[:, 0:P], dv[:, 0, cols])
                        mm(B[7][:, cols], dPT[:, P:2 * P], dv[:, 0, cols], stop=False)
                        mm(B[7][:, cols], dPT[:, 2 * P:3 * P], dv[:, 1, cols], start=False).then_inc(s_dil_pv, 1)
                    if 0 <= h - 1 < DH:
                        pe.wait_ge(s_dil_exp, DH * l + h)
                        for i3 in range(3):
                            last = nc.tensor.transpose(B[5][:, P * i3:P * i3 + P], dL[:, P * i3:P * i3 + P], ident)
                        last.then_inc(s_dil_p_T, 1)
                    if 0 <= h < DH:
                        if h == 0:
                            pe.wait_ge(s_dil_kT, l + 1)
                        r0, a = DE * (h % 2), h // 2
                        mm(B[4][:, 0:P], dqT[r0:r0 + DE, a, 0:P], dkT[r0:r0 + DE, a, 0:P])
                        mm(B[4][:, P:3 * P], dqT[r0:r0 + DE, a, P:2 * P], dkT[r0:r0 + DE, a, :]).then_inc(s_dil_scores, 1)
                    if k in (22, 24):
                        src, g = (T1, G_MQ) if k == 22 else (T0, G_MK)
                        if k == 22:
                            pe.wait_ge(s_group_out, G_GATE * l + (g + 1))
                        else:
                            pe.wait_ge(s_conv_in, 2 * l + 1)
                        if k == 22:
                            pe.wait_ge(s_dil_pT, DH * l + DH)
                        for tt in range(TT):
                            last = four_transposes(B[4 + tt], src[:, tt, :])
                        last.then_inc(s_ml_q_T if k == 22 else s_ml_k_T, 1)
                    if k == 23:
                        pe.wait_ge(s_dil_y, l + 1)
                        pe.wait_ge(s_ml_rows_exp, l + 1)
                        for hh in range(MH):
                            last = mm(B[7][:, 4 * hh:4 * hh + NC], cst[0:MH, C_SEL + P * hh:C_SEL + P * hh + P],
                                      WI[:, LC - 1:SEQ:LC])
                        for tt in range(TT):
                            for q, row in enumerate((G_, WI, WK, EM)):
                                col = 4 * (4 * tt + q)
                                last = nc.tensor.transpose(B[6][:, col:col + MH], row[:, P * tt:P * tt + P],
                                                           ident[0:MH, 0:MH])
                        last.then_inc(s_ml_cols, 1)
                    if k == 25:
                        pe.wait_ge(s_conv_in, 2 * l + 2)
                        for tt in range(TT):
                            for hh in range(MH):
                                last = mm(B[4 + tt][:, P * hh:P * hh + P],
                                          cst[0:MH, C_SEL + P * hh:C_SEL + P * hh + P], M_[:, P * tt:P * tt + P])
                        last.then_inc(s_ml_max_b, 1)
                    if k == 27:
                        pe.wait_ge(s_ml_weights, l + 1)
                        for tt in range(TT):
                            tok = slice(P * tt, P * tt + P)
                            for hh in range(MH):
                                last = mm(B[4 + tt][:, P * hh:P * hh + P], qkT[:, MH + hh, tok], qkT[:, hh, tok])
                        last.then_inc(s_ml_scores, 1)
                        pe.wait_ge(s_ml_mc, l + 1)
                        for tt in range(TT):
                            for hh in range(MH):
                                last = nc.tensor.transpose(B[6 + tt][:, P * hh:P * hh + P],
                                                           qkT[:, MH + hh, P * tt:P * tt + P], ident)
                        last.then_inc(s_ml_k_nat, 1)
                    if k == 28:
                        pe.wait_ge(s_ml_A, l + 1)
                        for hh in range(MH):
                            last = mm(B[4 + hh // 2][:, SEQ * (hh % 2):SEQ * (hh % 2) + SEQ],
                                      cst[0:MH, C_SEL + P * hh:C_SEL + P * hh + P], WI)
                        last.then_inc(s_ml_inter_b, 1)
                    if k in (29, 30):
                        h0 = 0 if k == 29 else 2
                        if k == 29:
                            pe.wait_ge(s_ml_q, l + 1)
                        else:
                            pe.wait_ge(s_ml_state, 2 * l + 1)
                        for hh in range(2):
                            for c in range(NC - 1):
                                tt, r0 = c // 2, LC * (c % 2)
                                last = mm(B[(6, 7, 4)[c]][:, (ME + 1) * hh:(ME + 1) * (hh + 1)],
                                          mkw[r0:r0 + LC, tt, P * (h0 + hh):P * (h0 + hh) + P],
                                          mv1[r0:r0 + LC, tt, h0 + hh, :])
                        last.then_inc(s_ml_kv, 1)

                pe.wait_ge(s_gates_out, GATE_GRPS * l + (GATE_GRPS - 1))
                for tt in range(TT):
                    last = four_transposes(B[tt], gr[:, tt, :])
                last.then_inc(s_yT, 1)
                pe.wait_ge(s_ml_state, 2 * l + 2)
                for tt in range(TT):
                    for hh in range(MH):
                        col = (ME + 1) * (hh % 2)
                        bank = B[4 + 2 * tt + hh // 2]
                        last = mm(bank[:, col:col + ME + 1], mA[:, tt, P * hh:P * hh + P], mv1[:, tt, hh, :], stop=False)
                        for c in (2 * tt, 2 * tt + 1):
                            if c:
                                o0 = LC * (c % 2)
                                last = mm(bank[o0:o0 + LC, col:col + ME + 1], qwT[:, hh, LC * c:LC * c + LC],
                                          mcs[:, c - 1, hh, :], start=False)
                    last.then_inc(s_ml_out, 1)
                pe.wait_ge(s_gates_out, GATE_GRPS * l + GATE_GRPS)
                for tt in range(TT):
                    last = four_transposes(B[2 + tt], T1[:, tt, :])
                last.then_inc(s_yT, 1)

                def project(b, j, c0):
                    layer_block(l, B_PROJ + 2 * b + j, (B[2 * j][:, :], B[2 * j + 1][:, :]), c0, True, True)

                pe.wait_ge(s_y_lo, 3 * l + 1)
                project(0, 0, 0)
                pe.wait_ge(s_y_lo, 3 * l + 2)
                project(0, 1, 0)
                pe.wait_ge(s_merged, 6 * l + 1)
                project(1, 0, 4)
                pe.wait_ge(s_ml_y, l + 1)
                for tt in range(TT):
                    last = four_transposes(B[4 + tt], mo[:, tt, :])
                last.then_inc(s_yT, 1)
                pe.wait_ge(s_merged, 6 * l + 2)
                project(1, 1, 4)
                pe.wait_ge(s_y_lo, 3 * l + 3)
                pe.wait_ge(s_merged, 6 * l + 3)
                project(2, 0, 0)

                def transpose_merged(j):
                    pe.wait_ge(s_merged, 6 * l + (j + 5))
                    for tt in range(TT):
                        last = four_transposes(B[2 * j + tt], gates[:, tt, 512 * j:512 * j + 512])
                    last.then_inc(s_merged_T, 1)

                pe.wait_ge(s_merged, 6 * l + 4)
                pe.wait_ge(s_lo, BLOCKS * l + (B_PROJ + 6))
                for tt in range(TT):
                    ins = wide_tile((B_PROJ + 5) % SLOTS, B[2 + tt][:, :], tt, 0, True, True)
                    if tt == 0:
                        transpose_merged(0)
                ins.then_inc(s_used, 1)
                pe.wait_ge(s_merged_lo, 2 * l + 1)
                for j in range(2):
                    layer_block(l, B_OUT + j, (B[4 + j][:, :], B[6 + j][:, :]), 4, True, False)
                    if j == 0:
                        transpose_merged(1)
                pe.wait_ge(s_merged_lo, 2 * l + 2)
                pe.wait_ge(s_lo, BLOCKS * l + (B_OUT + 4))
                for tt in range(TT):
                    for j in range(2):
                        ins = wide_tile((B_OUT + 2 + j) % SLOTS, B[4 + 2 * tt + j][:, :], tt, 0, False, True)
                        ins.then_inc(s_used if tt else s_acc, 1)
                transpose_x(3 * l + 2, 0)
                ffn(l, 1, B_FFN2, 3 * l + 2)


def shape_constants():
    c = np.zeros((P, C_W), np.float32)
    s, t = np.arange(P)[:, None], np.arange(P)[None, :]
    same = s // LC == t // LC
    c[:, C_ID:C_ID + P] = s == t
    c[:, C_TRI:C_TRI + P] = same & (s <= t)
    c[:, C_SUF:C_SUF + P] = same & (s > t)
    c[:, C_OFF:C_OFF + P] = ~(same & (s <= t))
    q = np.arange(P)[:, None]
    dist = np.concatenate([q - t, q + P - np.arange(SEQ)[None, :]], axis=1)
    count = sum(((dist % dil == 0) & (dist <= window)).astype(int) for window, dil in
                ((128, 1), (512, 4), (2048, 16)))
    count = np.where(dist >= 0, count, 0)
    c[:, C_DIST:C_DIST + 384] = dist
    c[:, C_LNC:C_LNC + 384] = np.where(count > 0, np.log(np.maximum(count, 1)), -BIG)
    for h in range(MH):
        c[h, C_SEL + P * h:C_SEL + P * h + P] = 1.0
    return c


def weight_stream(inputs):
    s = np.empty((LAYERS, BLOCKS, P, BW), np.float32)

    def wide(w, c0, cols):
        return w[P * c0:P * c0 + 4 * P, cols].reshape(4, P, 512).transpose(1, 0, 2).reshape(P, BW)

    def down(w, g):
        return w[2 * P * g:2 * P * g + 2 * P].reshape(2, P, D).transpose(1, 0, 2).reshape(P, BW)

    widths = (256, 256, 512, 512, 16, 512, 512, 512, 512, 512, 512, 4, 4, 512, 3 * D)
    at = [0]
    for w in widths:
        at.append(at[-1] + w)
    gq, _, gv, gr, _, dq, dk, dv, mq, mk, mv, _, _, mo, gates, _ = at
    groups = [gq, gv, gr, dq, dk, dv, mq, mk, mv, mo] + [gates + 512 * i for i in range(6)]
    for l in range(LAYERS):
        for f, base in ((1, 0), (2, B_FFN2)):
            wg, wu, wd = (np.asarray(inputs[f"ffn{f}_w_{n}"])[l] for n in ("gate", "up", "down"))
            for g in range(NG):
                gu = np.concatenate([wg[:, FG * g:FG * g + FG], wu[:, FG * g:FG * g + FG]], axis=1)
                n = base if g == 0 else base + SLOTS * g - 1
                s[l, n], s[l, n + 1] = wide(gu, 0, slice(0, 512)), wide(gu, 4, slice(0, 512))
                s[l, base + SLOTS * g + 4 if g < NG - 1 else base + FB - 1] = down(wd, g)
        w = np.asarray(inputs["w_in"])[l]
        for i, c in enumerate(groups):
            for k in range(2):
                s[l, B_MIX + 2 * i + k] = wide(w, 4 * k, slice(c, c + 512))
        for b, n in enumerate(("gla", "dil", "ml")):
            w = np.asarray(inputs[f"w_proj_{n}"])[l]
            for j in range(2):
                s[l, B_PROJ + 2 * b + j] = wide(w, 0, slice(512 * j, 512 * j + 512))
        w = np.asarray(inputs["w_out"])[l]
        for c in range(2):
            for j in range(2):
                s[l, B_OUT + 2 * c + j] = wide(w, 4 * c, slice(512 * j, 512 * j + 512))
    return s.reshape(LAYERS * BLOCKS, P, BW)


def kernel(**inputs):
    import concourse.bacc as _bacc
    from concourse.bass_utils import run_bass_kernel_spmd as _run

    a = {n: np.asarray(v) for n, v in inputs.items()}
    w_in = a["w_in"].reshape(LAYERS, KD, P, -1)
    wsmall = np.zeros((LAYERS, P, KD, SM), np.float32)
    wsmall[..., 0:16] = w_in[..., 1536:1552].transpose(0, 2, 1, 3)
    wsmall[..., 32:36] = w_in[..., 4624:4628].transpose(0, 2, 1, 3)
    wsmall[..., 64:68] = w_in[..., 4628:4632].transpose(0, 2, 1, 3)
    conv = np.concatenate([a["ml_conv_w"], a["ml_conv_b"][:, None, :]], axis=1)
    arrays = {
        "x": a["x"].reshape(SEQ, D),
        "stream": weight_stream(inputs),
        "consts": shape_constants(),
        "lnp": np.stack([np.concatenate([a[f"ln{i}_g"], a[f"ln{i}_b"]], axis=1) for i in (1, 2, 3)], axis=1),
        "vecs": np.concatenate([a["gla_norm_g"], a["ml_norm_g"], a["gla_b_a"]], axis=1),
        "bgate": a["b_gate"],
        "wsmall": wsmall.reshape(LAYERS, P, KD * SM),
        "wa2": a["gla_w_a2"],
        "bif": np.stack([a["ml_b_i"], a["ml_b_f"]], axis=2),
        "convp": conv.reshape(LAYERS, CONV + 1, 2 * MH, P).transpose(0, 3, 2, 1),
    }
    arrays = {n: np.ascontiguousarray(v) for n, v in arrays.items()}
    nc = _bacc.Bacc("TRN2", target_bir_lowering=False, num_devices=1)
    args = [nc.dram_tensor(n, v.shape, F32, kind="ExternalInput").ap() for n, v in arrays.items()]
    out = nc.dram_tensor("out", (SEQ, D), F32, kind="ExternalOutput").ap()
    trunk(nc, *args, out)
    r = _run(nc, [arrays], core_ids=[0])
    return r.results[0]["out"].reshape(1, SEQ, D)
```
